# Optimizing a Trainium2 kernel written in Bass

```python
import jax, jax.numpy as jnp
from jax import lax
import numpy as np

D_MODEL = 1024
BATCH = 1
SEQ = 1024
DEPTH = 2
DEC_BATCH = 1
DEC_SEQ = 32
PAST_LEN = 256

CHUNK = 64
N_AB_LAYERS = (DEPTH + 1) // 2
N_C_LAYERS = DEPTH // 2
A_WIDTH = D_MODEL // 2
B_WIDTH = D_MODEL // 2
B_GROUPS = 8
B_HEAD_DIM = B_WIDTH // B_GROUPS
GMLP_CHUNK = 128
CONV_A_WIDTH = 31
C_WIDTH = D_MODEL
CONV_C_WIDTH = 3
D_FF = 2816
CONV_F_WIDTH = 3
EPS = 1e-6

kernel_name = "hybrid_streaming_conv_gmlp_encoder_step"

def rmsnorm(x, g):
    xf = x.astype(jnp.float32)
    y = xf * lax.rsqrt(jnp.mean(xf * xf, axis=-1, keepdims=True) + EPS)
    return (y * g.astype(jnp.float32)).astype(x.dtype)

def layernorm(x, g, b):
    xf = x.astype(jnp.float32)
    mu = jnp.mean(xf, axis=-1, keepdims=True)
    xc = xf - mu
    y = xc * lax.rsqrt(jnp.mean(xc * xc, axis=-1, keepdims=True) + EPS)
    return (y * g.astype(jnp.float32) + b.astype(jnp.float32)).astype(x.dtype)

def causal_dwconv(x, past, w):
    width = w.shape[0]
    xp = jnp.concatenate([past.astype(x.dtype), x], axis=1)
    y = lax.conv_general_dilated(xp, w[:, None, :].astype(x.dtype), window_strides=(1,), padding="VALID",
                                 dimension_numbers=("NWC", "WIO", "NWC"), feature_group_count=x.shape[-1])
    return y, xp[:, xp.shape[1] - (width - 1):]

def chunk_mask(length):
    i = jnp.arange(length)
    return (i[None, :] // CHUNK) <= (i[:, None] // CHUNK)

def spatial_gating(u, v, ws, bs):
    bsz, t, _ = v.shape
    length = min(t, GMLP_CHUNK)
    n = t // length
    w = jnp.where(chunk_mask(length)[None], ws[:, :length, :length], 0.0)
    vc = v.reshape(bsz, n, length, B_GROUPS, B_HEAD_DIM)
    s = jnp.einsum("gij,bnjgd->bnigd", w, vc) + bs[:, :length].T[None, None, :, :, None]
    return u * s.reshape(bsz, t, B_WIDTH)

def mixer_ab(h, past_a, w_in, conv_w, conv_b, lna_g, lna_b, lnv_g, lnv_b, ws, bs, w_out):
    z = h @ w_in
    a_val, a_gate, u, v = jnp.split(z, [A_WIDTH, 2 * A_WIDTH, 2 * A_WIDTH + B_WIDTH], axis=-1)
    a = a_val * jax.nn.sigmoid(a_gate)
    a_conv, new_past_a = causal_dwconv(a, past_a, conv_w)
    a_out = jax.nn.silu(layernorm(a_conv + conv_b, lna_g, lna_b))
    v = layernorm(v, lnv_g, lnv_b)
    b_out = spatial_gating(u, v, ws, bs)
    y = jnp.concatenate([a_out, b_out], axis=-1) @ w_out
    return y, new_past_a, v

def mixer_c(h, past_c, w_in, conv_w, w_out):
    z = h @ w_in
    bg, cg, hx = jnp.split(z, 3, axis=-1)
    hc, new_past_c = causal_dwconv(cg * hx, past_c, conv_w)
    return (bg * hc) @ w_out, new_past_c

def conv_ffn(h, past_f, w_up, conv_w, w_down):
    z = h @ w_up
    g, up = jnp.split(z, 2, axis=-1)
    gc, new_past_f = causal_dwconv(g, past_f, conv_w)
    return (jax.nn.silu(gc) * up) @ w_down, new_past_f

def trunk(x, past_a, past_c, past_f, norm_mix, norm_ffn, norm_final, w_in_ab, conv_a_w, conv_a_b, ln_a_g, ln_a_b,
          ln_v_g, ln_v_b, ws_b, bs_b, w_out_ab, w_in_c, conv_c_w, w_out_c, w_up, conv_f_w, w_down):
    new_a, new_c, new_f, v_rows = [], [], [], []
    for l in range(DEPTH):
        h = rmsnorm(x, norm_mix[l])
        i = l // 2
        if l % 2 == 0:
            y, pa, v = mixer_ab(h, past_a[i], w_in_ab[i], conv_a_w[i], conv_a_b[i], ln_a_g[i], ln_a_b[i],
                                ln_v_g[i], ln_v_b[i], ws_b[i], bs_b[i], w_out_ab[i])
            new_a.append(pa)
            v_rows.append(v)
        else:
            y, pc = mixer_c(h, past_c[i], w_in_c[i], conv_c_w[i], w_out_c[i])
            new_c.append(pc)
        x = x + y
        h = rmsnorm(x, norm_ffn[l])
        y, pf = conv_ffn(h, past_f[l], w_up[l], conv_f_w[l], w_down[l])
        new_f.append(pf)
        x = x + y
    return rmsnorm(x, norm_final), jnp.stack(new_a), jnp.stack(new_c), jnp.stack(new_f), jnp.stack(v_rows)

def setup_inputs(seed: int = 0) -> dict:
    key = jax.random.key(seed)
    ks = jax.random.split(key, 24)
    nrm = jax.random.normal
    f32 = jnp.float32
    d = D_MODEL
    return {
        "x_prompt": nrm(ks[0], (BATCH, SEQ, d), f32),
        "x_sample": nrm(ks[1], (DEC_BATCH, DEC_SEQ, d), f32),
        "state_conv_a": 0.5 * nrm(ks[2], (N_AB_LAYERS, DEC_BATCH, CONV_A_WIDTH - 1, A_WIDTH), f32),
        "state_conv_c": nrm(ks[3], (N_C_LAYERS, DEC_BATCH, CONV_C_WIDTH - 1, C_WIDTH), f32),
        "state_ffn": nrm(ks[4], (DEPTH, DEC_BATCH, CONV_F_WIDTH - 1, D_FF), f32),
        "norm_mix": 1.0 + 0.05 * nrm(ks[5], (DEPTH, d), f32),
        "norm_ffn": 1.0 + 0.05 * nrm(ks[6], (DEPTH, d), f32),
        "norm_final": 1.0 + 0.05 * nrm(ks[7], (d,), f32),
        "w_in_ab": nrm(ks[8], (N_AB_LAYERS, d, 2 * A_WIDTH + 2 * B_WIDTH), f32) * d ** -0.5,
        "conv_a_w": nrm(ks[9], (N_AB_LAYERS, CONV_A_WIDTH, A_WIDTH), f32) * CONV_A_WIDTH ** -0.5,
        "conv_a_b": 0.02 * nrm(ks[10], (N_AB_LAYERS, A_WIDTH), f32),
        "ln_a_g": 1.0 + 0.05 * nrm(ks[11], (N_AB_LAYERS, A_WIDTH), f32),
        "ln_a_b": 0.02 * nrm(ks[12], (N_AB_LAYERS, A_WIDTH), f32),
        "ln_v_g": 1.0 + 0.05 * nrm(ks[13], (N_AB_LAYERS, B_WIDTH), f32),
        "ln_v_b": 0.02 * nrm(ks[14], (N_AB_LAYERS, B_WIDTH), f32),
        "ws_b": nrm(ks[15], (N_AB_LAYERS, B_GROUPS, GMLP_CHUNK, GMLP_CHUNK), f32) * GMLP_CHUNK ** -0.5,
        "bs_b": 1.0 + 0.05 * nrm(ks[16], (N_AB_LAYERS, B_GROUPS, GMLP_CHUNK), f32),
        "w_out_ab": nrm(ks[17], (N_AB_LAYERS, A_WIDTH + B_WIDTH, d), f32) * (A_WIDTH + B_WIDTH) ** -0.5,
        "w_in_c": nrm(ks[18], (N_C_LAYERS, d, 3 * C_WIDTH), f32) * d ** -0.5,
        "conv_c_w": nrm(ks[19], (N_C_LAYERS, CONV_C_WIDTH, C_WIDTH), f32) * CONV_C_WIDTH ** -0.5,
        "w_out_c": nrm(ks[20], (N_C_LAYERS, C_WIDTH, d), f32) * C_WIDTH ** -0.5,
        "w_up": nrm(ks[21], (DEPTH, d, 2 * D_FF), f32) * d ** -0.5,
        "conv_f_w": nrm(ks[22], (DEPTH, CONV_F_WIDTH, D_FF), f32) * CONV_F_WIDTH ** -0.5,
        "w_down": nrm(ks[23], (DEPTH, D_FF, d), f32) * D_FF ** -0.5,
    }

def reference(x_prompt, x_sample, state_conv_a, state_conv_c, state_ffn, norm_mix, norm_ffn, norm_final,
              w_in_ab, conv_a_w, conv_a_b, ln_a_g, ln_a_b, ln_v_g, ln_v_b, ws_b, bs_b, w_out_ab,
              w_in_c, conv_c_w, w_out_c, w_up, conv_f_w, w_down):
    bp = x_prompt.shape[0]
    dt = x_prompt.dtype
    past_a_p = [jnp.zeros((bp, CONV_A_WIDTH - 1, A_WIDTH), dt) for _ in range(N_AB_LAYERS)]
    past_c_p = [jnp.zeros((bp, CONV_C_WIDTH - 1, C_WIDTH), dt) for _ in range(N_C_LAYERS)]
    past_f_p = [jnp.zeros((bp, CONV_F_WIDTH - 1, D_FF), dt) for _ in range(DEPTH)]
    y_prompt, new_conv_a_prompt, new_conv_c_prompt, new_ffn_prompt, _ = trunk(
        x_prompt, past_a_p, past_c_p, past_f_p, norm_mix, norm_ffn, norm_final, w_in_ab, conv_a_w, conv_a_b,
        ln_a_g, ln_a_b, ln_v_g, ln_v_b, ws_b, bs_b, w_out_ab, w_in_c, conv_c_w, w_out_c, w_up, conv_f_w, w_down)
    past_a_s = [state_conv_a[i] for i in range(N_AB_LAYERS)]
    past_c_s = [state_conv_c[i] for i in range(N_C_LAYERS)]
    past_f_s = [state_ffn[l] for l in range(DEPTH)]
    y_sample, new_conv_a_sample, new_conv_c_sample, new_ffn_sample, new_gmlp_v_sample = trunk(
        x_sample, past_a_s, past_c_s, past_f_s, norm_mix, norm_ffn, norm_final, w_in_ab, conv_a_w, conv_a_b,
        ln_a_g, ln_a_b, ln_v_g, ln_v_b, ws_b, bs_b, w_out_ab, w_in_c, conv_c_w, w_out_c, w_up, conv_f_w, w_down)
    return (y_prompt, y_sample, new_conv_a_prompt, new_conv_a_sample, new_conv_c_prompt, new_conv_c_sample,
            new_ffn_prompt, new_ffn_sample, new_gmlp_v_sample)


_drawn_inputs = setup_inputs


def setup_inputs(seed=0):
    import zlib

    import numpy as np

    out = dict(_drawn_inputs(seed))
    spreads = {}
    factors = {'conv_a_b': 2.819, 'ln_a_b': 5.895, 'ln_v_b': 3.01}
    for name, (base, spread) in spreads.items():
        noise = np.random.default_rng([zlib.crc32(name.encode()), seed]).standard_normal(out[name].shape)
        drawn = base * np.exp(spread * noise) if base else spread * noise
        out[name] = __import__('jax').numpy.asarray(drawn.astype(out[name].dtype))
    for name, factor in factors.items():
        out[name] = (out[name] * factor).astype(out[name].dtype)
    return out
```

```python
import numpy as np

import concourse.bass as bass
from concourse import mybir
from contextlib import ExitStack

F32 = mybir.dt.float32
F32R = mybir.dt.float32r
ALU = mybir.AluOpType
ACT = mybir.ActivationFunctionType

P = 128
D = 1024
SEQ = 1024
DEC = 32
DFF = 2816
AW = 512
TAPS_A = 31
EPS = 1e-6

KD = D // P
SAMPLE = SEQ + 2
COLS = 1062
CH = COLS // 3
ROW_TILES = 9
FF_TILES = DFF // P
FF_BLOCKS = FF_TILES // 2
SLAB = 8 * P

HA = TAPS_A - 1
A_COLS = HA + SEQ + HA + DEC
AO_COLS = A_COLS - HA
AO_SAMPLE = SEQ + HA
POOL_TAPS = 10
DVE_TAPS = TAPS_A - POOL_TAPS

_SIZES = [("gain", 5 * KD), ("conv_a_w", 4 * TAPS_A), ("conv_a_b", 4), ("ln_a_g", 4), ("ln_a_b", 4),
          ("state_a", 4 * HA), ("conv_c_w", KD * 3), ("state_c", KD * 2),
          ("conv_f_w", 2 * FF_TILES * 3), ("state_f", 2 * FF_TILES * 2)]
OFF = {}
_at = 0
for _name, _size in _SIZES:
    OFF[_name] = _at
    _at += _size
N_CONST = _at

AB_SLABS = 24
JOB_A = [0, 2, 12, 14]
JOB_V = [4, 5, 7, 9]
JOB_VT = [6, 8, 10, 11]
JOB_S = [16, 18, 20, 22]
JOB_DOWN_B = 24
JOB_LN = 32
JOB_DOWN_A = 33
AB_JOBS = 41
FF_SLABS = 6 * FF_BLOCKS
FF_JOBS = 12 * FF_BLOCKS
C_SLABS = 32
C_JOBS = 56

JOB0 = [0, AB_JOBS, AB_JOBS + FF_JOBS, AB_JOBS + FF_JOBS + C_JOBS]
SLAB0 = [0, AB_SLABS, AB_SLABS + FF_SLABS, AB_SLABS + FF_SLABS + C_SLABS]
N_SLABS = AB_SLABS + 2 * FF_SLABS + C_SLABS
N_JOBS = JOB0[3] + FF_JOBS


def _jobs_after_slab():
    after = []
    for c in (0, 1):
        after += [JOB_A[c] + 1, JOB_A[c] + 2]
    after += [j + 1 for j in JOB_V]
    for c in (2, 3):
        after += [JOB_A[c] + 1, JOB_A[c] + 2]
    after += [j + 2 for j in JOB_S]
    after += [JOB_DOWN_B + 2 * (s + 1) for s in range(4)]
    after += [JOB_DOWN_A + 2 * (s + 1) for s in range(4)]
    for phase in (1, 2, 3):
        at = JOB0[phase]
        if phase == 2:
            steps = ([1] * 12 + [4] * 4) * 2
        else:
            steps = [1] * 4 + ([1] * 4 + [4, 4]) * (FF_BLOCKS - 1) + [4, 4]
        for s in steps:
            at += s
            after.append(at)
    return after


AFTER = _jobs_after_slab()

ACT0 = [0, 8, 8 + FF_TILES, 8 + FF_TILES + KD]
CONV0 = [None, 0, FF_TILES, FF_TILES + KD]


def build(nc, x_in, slabs, consts_in, mix_in, bs_in, lnv_in, y_out, a_state, c_state, f_state, v_out):
    with ExitStack() as ctx:
        def sb(name, cols, dt=F32):
            return ctx.enter_context(nc.sbuf_tensor(name, [P, cols], dt))

        def sem(name):
            return ctx.enter_context(nc.semaphore(name))

        x = sb("x", KD * COLS)
        xg_hi = sb("xg_hi", KD * COLS, F32R)
        xg_lo = sb("xg_lo", KD * COLS, F32R)
        act_hi = sb("act_hi", 4 * COLS, F32R)
        act_lo = sb("act_lo", 4 * COLS, F32R)
        raw = sb("raw", 2 * SLAB)
        w_hi = sb("w_hi", 2 * SLAB, F32R)
        w_lo = sb("w_lo", 2 * SLAB, F32R)
        r_rows = sb("r_rows", COLS)
        sumsq = sb("sumsq", ROW_TILES * P)
        work = sb("work", 5 * A_COLS + 2 * COLS + AO_COLS)
        const = sb("const", N_CONST)
        ident = sb("ident", P)
        ones = sb("ones", 1)
        minus_half = sb("minus_half", ROW_TILES)
        mean_sq = sb("mean_sq", ROW_TILES)
        r_col = sb("r_col", ROW_TILES)
        bn = sb("bn", ROW_TILES * 6)
        mv = sb("mv", ROW_TILES * 2)
        var_eps = sb("var_eps", ROW_TILES)
        rstd = sb("rstd", ROW_TILES)
        neg_mean = sb("neg_mean", ROW_TILES)
        new_a = sb("new_a", 4 * 2 * HA)
        new_c = sb("new_c", KD * 4)
        new_f = sb("new_f", 2 * FF_TILES * 4)
        psum = ctx.enter_context(nc.psum_tensor("psum", [P, 8, 512], F32))

        def cst(name, at, n=1):
            return const[:, bass.ds(OFF[name] + at, n)]

        x_t = x[:].rearrange("p (m n) -> p m n", m=KD)
        hi_t = xg_hi[:].rearrange("p (m n) -> p m n", m=KD)
        lo_t = xg_lo[:].rearrange("p (m n) -> p m n", m=KD)
        ah_t = act_hi[:].rearrange("p (m n) -> p m n", m=4)
        al_t = act_lo[:].rearrange("p (m n) -> p m n", m=4)
        r_3 = r_rows[:].rearrange("p (c n) -> p c n", c=3)

        GW = COLS + 2
        conv_in = [work[:, i * GW:(i + 1) * GW] for i in range(2)]
        conv_out = [work[:, (2 + i) * GW:(2 + i) * GW + COLS] for i in range(2)]
        factor = [work[:, (4 + i) * GW:(4 + i) * GW + COLS] for i in range(2)]
        prod = [work[:, (6 + i) * GW:(6 + i) * GW + COLS] for i in range(2)]
        square = [work[:, i * GW:i * GW + COLS] for i in range(2)]
        A_IN = [0, 1, 2, 3]
        A_OUT = [4, 0, 1, 2]
        a_in = [work[:, b * A_COLS:(b + 1) * A_COLS] for b in A_IN]
        a_out = [work[:, b * A_COLS:b * A_COLS + AO_COLS] for b in A_OUT]
        tmp = [work[:, 5 * A_COLS + i * COLS:5 * A_COLS + (i + 1) * COLS] for i in range(2)]
        tap_prod = [sumsq[:, 0:AO_COLS], work[:, 5 * A_COLS + 2 * COLS:5 * A_COLS + 2 * COLS + AO_COLS]]
        v_rows = x[:, 0:ROW_TILES * AW].rearrange("p (t f) -> p t f", t=ROW_TILES)
        at = ROW_TILES * AW
        mix_w = x[:, at:at + 8 * P].rearrange("p (g i) -> p g i", g=8)
        at += 8 * P
        mix_b = x[:, at:at + 4 * P].rearrange("p (c i) -> p c i", c=4)
        at += 4 * P
        lnv_g = x[:, at:at + AW]
        lnv_b = x[:, at + AW:at + 2 * AW]
        assert at + 2 * AW <= KD * COLS - AO_COLS
        pool_sum = x[:, KD * COLS - AO_COLS:KD * COLS]

        const_loaded = sem("const_loaded")
        x_loaded = [sem(f"x_loaded{m}") for m in range(KD)]
        mix_loaded = sem("mix_loaded")
        raw_loaded = [sem(f"raw_loaded{i}") for i in range(2)]
        weights_hi = sem("weights_hi")
        weights_ready = sem("weights_ready")
        consts_made = sem("consts_made")
        pad_cleared = sem("pad_cleared")
        tile_done = sem("tile_done")
        tile_evacuated = sem("tile_evacuated")
        xg_hi_ready = sem("xg_hi_ready")
        xg_ready = sem("xg_ready")
        square_ready = sem("square_ready")
        squares_summed = sem("squares_summed")
        stats_ready = sem("stats_ready")
        mean_sq_ready = sem("mean_sq_ready")
        r_col_ready = sem("r_col_ready")
        r_spread = sem("r_spread")
        r_ready = sem("r_ready")
        state_saved = sem("state_saved")
        history_set = sem("history_set")
        conv_tap = sem("conv_tap")
        factor_ready = sem("factor_ready")
        product_done = sem("product_done")
        act_hi_ready = sem("act_hi_ready")
        act_ready = sem("act_ready")
        sigmoid_done = sem("sigmoid_done")
        glu_written = sem("glu_written")
        a_tap = sem("a_tap")
        a_tap_product = sem("a_tap_product")
        a_pool_sum = sem("a_pool_sum")
        a_conv_done = sem("a_conv_done")
        a_rows_ready = sem("a_rows_ready")
        row_stats = sem("row_stats")
        row_moments = sem("row_moments")
        var_ready = sem("var_ready")
        rstd_ready = sem("rstd_ready")
        neg_mean_ready = sem("neg_mean_ready")
        v_scaled = sem("v_scaled")
        v_ready = sem("v_ready")
        mask_set = sem("mask_set")
        a_scaled = sem("a_scaled")
        a_normed = sem("a_normed")
        silu_done = sem("silu_done")
        y_ready = sem("y_ready")
        v_stored = sem("v_stored")
        stored = sem("stored")

        block = ctx.enter_context(nc.Block())

        @block.sync
        def _(sp):
            def load_slab(n, slot):
                sp.dma_start(raw[:, slot * SLAB:(slot + 1) * SLAB],
                             slabs[bass.ds(n, 1), :, :].rearrange("s p n -> p (s n)")).then_inc(raw_loaded[slot], 16)

            def load_slabs(first, end):
                for n in range(first, end):
                    sp.wait_ge(weights_ready, n - 1)
                    load_slab(n, n % 2)

            def load_x(m):
                sp.dma_start(x_t[:, m, :], x_in[m * P:(m + 1) * P, :]).then_inc(x_loaded[m], 16)

            load_slab(0, 0)
            load_x(0)
            sp.dma_start(const[:], consts_in).then_inc(const_loaded, 16)
            for m in range(1, KD):
                load_x(m)
                if m == 2:
                    load_slab(1, 1)
            load_slabs(2, 4)
            sp.wait_ge(xg_ready, KD)
            sp.wait_ge(squares_summed, KD - 1)
            sp.dma_start(mix_w, mix_in.rearrange("p (g i) -> p g i", g=8)).then_inc(mix_loaded, 16)
            sp.dma_start(mix_b, bs_in.rearrange("p (c i) -> p c i", c=4)).then_inc(mix_loaded, 16)
            sp.dma_start(x[:, at:at + 2 * AW], lnv_in).then_inc(mix_loaded, 16)
            load_slabs(4, 14)
            sp.wait_ge(v_ready, ROW_TILES)
            sp.dma_start(v_out, v_rows[0:DEC, ROW_TILES - 1, :]).then_inc(v_stored, 16)
            load_slabs(14, 17)
            sp.wait_ge(tile_evacuated, JOB_S[3] + 1)
            sp.wait_ge(v_stored, 16)
            for m in range(6):
                load_x(m)
            load_slabs(17, 20)
            sp.wait_ge(a_conv_done, 4)
            for m in (6, 7):
                load_x(m)
            sp.wait_ge(weights_ready, 19)
            load_slab(20, 0)
            sp.wait_ge(weights_ready, 20)
            load_slab(21, 1)
            sp.wait_ge(glu_written, 20)
            sp.dma_start(a_state, new_a[:]).then_inc(stored, 16)
            with sp.Fori(11, N_SLABS // 2) as i:
                sp.wait_ge(weights_ready, i * 2 - 1)
                load_slab(i * 2, 0)
                sp.wait_ge(weights_ready, i * 2)
                load_slab(i * 2 + 1, 1)
            sp.wait_ge(state_saved, 2 * FF_TILES + KD)
            sp.dma_start(c_state, new_c[:]).then_inc(stored, 16)
            sp.dma_start(f_state, new_f[:]).then_inc(stored, 16)
            for m in range(KD):
                sp.wait_ge(y_ready, m + 1)
                sp.dma_start(y_out[m * P:(m + 1) * P, :], x_t[:, m, :]).then_inc(stored, 16)
            sp.wait_ge(stored, 16 * (3 + KD))

        @block.tensor
        def _(pe):
            def split_product(out, w_at, slot, hi, lo, start, stop):
                s = slice(slot * SLAB + w_at * P, slot * SLAB + (w_at + 1) * P)
                nc.tensor.matmul(out, w_hi[:, s], hi, start=start, stop=False)
                nc.tensor.matmul(out, w_hi[:, s], lo, start=False, stop=False)
                return nc.tensor.matmul(out, w_lo[:, s], hi, start=False, stop=stop)

            def bank(pset, c):
                return psum[:, 3 * pset + c, 0:CH]

            def up_part(pset, slot, ks):
                for k in ks:
                    for c in range(3):
                        cols = slice(c * CH, (c + 1) * CH)
                        last = split_product(bank(pset, c), k, slot, hi_t[:, k, cols], lo_t[:, k, cols],
                                             k == 0, k == KD - 1)
                return last

            def up_job(job, slab, pset, slot, fresh=None):
                if not isinstance(job, int) or job >= 2:
                    pe.wait_ge(tile_evacuated, job - 1)
                pe.wait_ge(weights_ready, slab + 1)
                if fresh is None:
                    up_part(pset, slot, range(KD)).then_inc(tile_done, 1)
                else:
                    for k in range(KD):
                        pe.wait_ge(xg_ready, KD * fresh + k + 1)
                        last = up_part(pset, slot, [k])
                    last.then_inc(tile_done, 1)

            def down_jobs(job, slab, acts, act0, n_k, pset, slot):
                pe.wait_ge(weights_ready, slab + 1)
                for m in range(8 // n_k):
                    pe.wait_ge(tile_evacuated, job + m - 1)
                    for k in range(n_k):
                        if acts is not None and m == 0:
                            pe.wait_ge(act_ready, acts + k + 1)
                        for c in range(3):
                            cols = slice(c * CH, (c + 1) * CH)
                            last = split_product(bank((pset + m) % 2, c), m * n_k + k, slot,
                                                 ah_t[:, act0 + k, cols], al_t[:, act0 + k, cols],
                                                 k == 0, k == n_k - 1)
                    last.then_inc(tile_done, 1)

            def rms_stats(p, tail):
                pe.wait_ge(squares_summed, (KD - 1) * (p + 1))
                for t in range(ROW_TILES):
                    last = nc.tensor.matmul(psum[:, tail, CH + 2 + t:CH + 3 + t], sumsq[:, t * P:(t + 1) * P],
                                            ones[:], start=True, stop=True)
                last.then_inc(stats_ready, 1)

            def rms_spread(p, tail):
                pe.wait_ge(r_col_ready, p + 1)
                for t in range(ROW_TILES):
                    n = min(P, COLS - t * P)
                    out = psum[:, 6 + t // 4, (t % 4) * P:(t % 4 + 1) * P] if t < 8 else \
                        psum[:, tail, CH + 30:CH + 30 + n]
                    last = nc.tensor.matmul(out, r_col[:, t:t + 1].to_broadcast([P, P]), ident[:, 0:n],
                                            start=True, stop=True)
                last.then_inc(r_spread, 1)

            def phase_start(p):
                job, slab = JOB0[p], SLAB0[p]
                a, b = job % 2, (job + 1) % 2
                up_job(job, slab, a, slab % 2, fresh=p)
                rms_stats(p, 3 * a)
                if job:
                    pe.wait_ge(tile_evacuated, job)
                pe.wait_ge(weights_ready, slab + 2)
                up_part(b, (slab + 1) % 2, range(0, 5))
                rms_spread(p, 3 * a)
                up_part(b, (slab + 1) % 2, range(5, KD)).then_inc(tile_done, 1)

            def turn_v(c):
                job = JOB_VT[c]
                s = 3 * (job % 2)
                pe.wait_ge(tile_evacuated, JOB_V[c] + 1)
                pe.wait_ge(tile_evacuated, job - 1)
                for t in range(8):
                    nc.tensor.transpose(psum[:, s + t // 4, (t % 4) * P:(t % 4 + 1) * P],
                                        tmp[c % 2][:, t * P:(t + 1) * P], ident[:])
                nc.tensor.transpose(psum[0:DEC, s + 2, 0:P], tmp[c % 2][:, SAMPLE:SAMPLE + DEC],
                                    ident[:]).then_inc(tile_done, 1)

            def mix(job, pset, c):
                if not isinstance(job, int) or job >= 2:
                    pe.wait_ge(tile_evacuated, job - 1)
                for h in range(2):
                    g = 2 * c + h
                    rows = slice(64 * h, 64 * h + 64)
                    for n in range(8):
                        nc.tensor.matmul(psum[rows, 3 * pset + n // 4, (n % 4) * P:(n % 4 + 1) * P],
                                         v_rows[:, n, 64 * g:64 * g + 64], mix_w[:, g, :],
                                         start=True, stop=True)
                    last = nc.tensor.matmul(psum[rows, 3 * pset + 2, 0:DEC],
                                            v_rows[0:DEC, 8, 64 * g:64 * g + 64],
                                            mix_w[0:DEC, g, 0:DEC], start=True, stop=True)
                last.then_inc(tile_done, 1)

            def a_rows(t):
                pe.wait_ge(a_conv_done, 4)
                if t >= 2:
                    pe.wait_ge(row_stats, ROW_TILES + t - 1)
                n = P if t < 8 else DEC
                at_col = t * P if t < 8 else AO_SAMPLE
                for c in range(4):
                    last = nc.tensor.transpose(psum[0:n, 6 + t % 2, c * P:(c + 1) * P],
                                               a_out[c][:, at_col:at_col + n], ident[:])
                last.then_inc(a_rows_ready, 1)

            pe.wait_ge(consts_made, 4)
            phase_start(0)
            up_job(2, 2, 0, 0)
            up_job(3, 3, 1, 1)
            up_job(4, 4, 0, 0)
            up_job(5, 5, 1, 1)
            turn_v(0)
            up_job(7, 6, 1, 0)
            turn_v(1)
            up_job(9, 7, 1, 1)
            turn_v(2)
            turn_v(3)
            with pe.Fori(0, 2) as i:
                up_job(i * 2 + 12, i * 2 + 8, 0, 0)
                up_job(i * 2 + 13, i * 2 + 9, 1, 1)
            pe.wait_ge(v_ready, ROW_TILES)
            pe.wait_ge(mask_set, 1)
            for c in range(4):
                mix(JOB_S[c], 0, c)
                up_job(JOB_S[c] + 1, 12 + c, 1, c % 2)
            pe.wait_ge(act_ready, 4)
            with pe.Fori(0, 2) as i:
                down_jobs(i * 4 + JOB_DOWN_B, i * 2 + 16, None, 0, 4, 0, 0)
                down_jobs(i * 4 + JOB_DOWN_B + 2, i * 2 + 17, None, 0, 4, 0, 1)
            for t in range(ROW_TILES):
                a_rows(t)
            pe.wait_ge(neg_mean_ready, 1)
            pe.wait_ge(row_stats, 2 * ROW_TILES)
            pe.wait_ge(tile_evacuated, JOB_LN - 1)
            for t in range(ROW_TILES):
                k = P if t < 8 else DEC
                for col, b0, tail in ((rstd, 6, 0), (neg_mean, 0, DEC)):
                    out = psum[:, b0 + t // 4, (t % 4) * P:(t % 4 + 1) * P] if t < 8 else \
                        psum[:, 2, tail:tail + DEC]
                    last = nc.tensor.matmul(out, col[0:k, t:t + 1].to_broadcast([k, P]), ident[0:k, 0:k],
                                            start=True, stop=True)
            last.then_inc(tile_done, 1)
            down_jobs(JOB_DOWN_A, 20, 4, 0, 4, 1, 0)
            down_jobs(JOB_DOWN_A + 2, 21, None, 0, 4, 1, 1)
            down_jobs(JOB_DOWN_A + 4, 22, None, 0, 4, 1, 0)
            down_jobs(JOB_DOWN_A + 6, 23, None, 0, 4, 1, 1)

            def ffn(p):
                job, slab, act = JOB0[p], SLAB0[p], ACT0[p]
                s0 = job % 2
                phase_start(p)
                up_job(job + 2, slab + 2, s0, 0)
                up_job(job + 3, slab + 3, 1 - s0, 1)
                with pe.Fori(0, (FF_BLOCKS - 1) // 2) as i:
                    for q in range(2):
                        j = i * 24 + (job + 4 + 12 * q)
                        s = i * 12 + (slab + 4 + 6 * q)
                        for t in range(4):
                            up_job(j + t, s + t, (s0 + t) % 2, t % 2)
                        down_jobs(j + 4, s + 4, i * 4 + (act + 2 * q), 2 * q, 2, s0, 0)
                        down_jobs(j + 8, s + 5, None, 2 * q, 2, s0, 1)
                j, s = job + FF_JOBS - 8, slab + FF_SLABS - 2
                down_jobs(j, s, act + FF_TILES - 2, 0, 2, s0, 0)
                down_jobs(j + 4, s + 1, None, 0, 2, s0, 1)

            ffn(1)
            s0 = JOB0[2] % 2
            for half in range(2):
                job, slab = JOB0[2] + 28 * half, SLAB0[2] + 16 * half
                if half == 0:
                    phase_start(2)
                for t in range(0 if half else 2, 12):
                    up_job(job + t, slab + t, (s0 + t) % 2, t % 2)
                for q in range(2):
                    down_jobs(job + 12 + 8 * q, slab + 12 + 2 * q, ACT0[2] + 4 * half + 2 * q, 2 * q, 2, s0, 0)
                    down_jobs(job + 16 + 8 * q, slab + 13 + 2 * q, None, 2 * q, 2, s0, 1)
            ffn(3)
            rms_stats(4, 0)
            rms_spread(4, 0)

        @block.gpsimd
        def _(pool):
            nc.gpsimd.memset(ident[:], 0.0).then_inc(consts_made, 1)
            nc.gpsimd.memset(minus_half[:], -0.5).then_inc(consts_made, 1)
            nc.gpsimd.memset(ones[:], 1.0).then_inc(consts_made, 1)
            pool.wait_ge(consts_made, 3)
            nc.gpsimd.affine_select(out=ident[:], in_=ident[:], compare_op=ALU.not_equal, fill=1.0, base=0,
                                    pattern=[[-1, P]], channel_multiplier=1).then_inc(consts_made, 1)

            def split_lo(n, slot):
                pool.wait_ge(weights_hi, n + 1)
                s = slice(slot * SLAB, (slot + 1) * SLAB)
                nc.gpsimd.tensor_tensor(w_lo[:, s], raw[:, s], w_hi[:, s].bitcast(F32),
                                        ALU.subtract).then_inc(weights_ready, 1)

            def r_of_frames(p):
                pool.wait_ge(mean_sq_ready, p + 1)
                nc.gpsimd.tensor_tensor(r_col[:], mean_sq[:], minus_half[:], ALU.pow).then_inc(r_col_ready, 1)

            def pool_taps(c, first, end):
                for i in range(first, end):
                    if i == 0:
                        continue
                    pool.wait_ge(a_tap_product, POOL_TAPS * c + i + 1)
                    if i == 1:
                        if c:
                            pool.wait_ge(a_conv_done, c)
                        a = tap_prod[(POOL_TAPS * c) % 2]
                    else:
                        pool.wait_ge(a_pool_sum, (POOL_TAPS - 1) * c + i - 1)
                        a = pool_sum
                    nc.gpsimd.tensor_tensor(pool_sum, a, tap_prod[(POOL_TAPS * c + i) % 2],
                                            ALU.add).then_inc(a_pool_sum, 1)

            def row_rstd(n):
                pool.wait_ge(var_ready, n)
                nc.gpsimd.tensor_tensor(rstd[:], var_eps[:], minus_half[:], ALU.pow).then_inc(rstd_ready, 1)

            split_lo(0, 0)
            split_lo(1, 1)
            r_of_frames(0)
            split_lo(2, 0)
            for slot, c, first, end in A_PLAN:
                split_lo(slot + 1, (slot + 1) % 2)
                if c is not None:
                    pool_taps(c, first, end)
                if slot == 8:
                    row_rstd(1)
            row_rstd(2)
            split_lo(20, 0)
            with pool.Fori(0, 2) as i:
                split_lo(i * 2 + 21, 1)
                split_lo(i * 2 + 22, 0)
            split_lo(25, 1)
            for p in (1, 2, 3):
                r_of_frames(p)
                n0 = SLAB0[p] + 2
                n1 = SLAB0[p + 1] + 2 if p < 3 else N_SLABS
                with pool.Fori(0, (n1 - n0) // 2) as i:
                    split_lo(i * 2 + n0, 0)
                    split_lo(i * 2 + n0 + 1, 1)
            r_of_frames(4)

        @block.scalar
        def _(act):
            def split_hi(n, slot, after):
                act.wait_ge(raw_loaded[slot], n * 8 + (16 - 8 * slot))
                if after is not None:
                    act.wait_ge(tile_done, after)
                s = slice(slot * SLAB, (slot + 1) * SLAB)
                nc.scalar.activation(w_hi[:, s], raw[:, s], ACT.Copy).then_inc(weights_hi, 1)

            def hi(n):
                if n < N_SLABS:
                    split_hi(n, n % 2, AFTER[n - 2] if n >= 2 else None)

            def make_xg(p, m, job=None):
                if job is None:
                    act.wait_ge(x_loaded[m], 16)
                else:
                    act.wait_ge(tile_evacuated, job + 1)
                if p < 4:
                    nc.scalar.activation(hi_t[:, m, :], x_t[:, m, :], ACT.Identity,
                                         scale=cst("gain", p * KD + m)).then_inc(xg_hi_ready, 1)
                if m == 0:
                    act.wait_ge(pad_cleared, p + 1)
                    out = sumsq[:, 0:COLS]
                else:
                    if m >= 3:
                        act.wait_ge(squares_summed, (KD - 1) * p + m - 2)
                    out = square[m % 2]
                nc.scalar.activation(out, x_t[:, m, :], ACT.Square).then_inc(square_ready, 1)

            def hidden_hi(a, par, slot):
                act.wait_ge(product_done, a + 1)
                nc.scalar.activation(ah_t[:, slot, :], prod[par], ACT.Copy).then_inc(act_hi_ready, 1)

            def silu_gate(t, par):
                act.wait_ge(conv_tap, t * 3 + 3)
                nc.scalar.activation(factor[par], conv_out[par], ACT.Silu).then_inc(silu_done, 1)

            def tap_products(c, first, end):
                for i in range(first, end):
                    if i == 0:
                        act.wait_ge(glu_written, 4 * (c + 2))
                    n = POOL_TAPS - 1
                    used = n * c - 1 if i == 0 else n * c if i == 1 else n * c + 1 if i <= 3 else n * c + i - 2
                    if used > 0:
                        act.wait_ge(a_pool_sum, used)
                    k = DVE_TAPS + i
                    nc.scalar.activation(tap_prod[(POOL_TAPS * c + i) % 2], a_in[c][:, k:k + AO_COLS], ACT.Identity,
                                         scale=cst("conv_a_w", c * TAPS_A + k)).then_inc(a_tap_product, 1)

            def sigmoid_gate(c):
                act.wait_ge(tile_evacuated, JOB_A[c] + 2)
                nc.scalar.activation(tmp[1], tmp[1], ACT.Sigmoid).then_inc(sigmoid_done, 1)

            act.wait_ge(const_loaded, 16)
            hi(0)
            make_xg(0, 0)
            make_xg(0, 1)
            hi(1)
            for m in range(2, KD):
                make_xg(0, m)
            hi(2)
            for slot, c, first, end in A_PLAN:
                hi(slot + 1)
                if slot in (2, 4):
                    sigmoid_gate(slot // 2 - 1)
                if slot in (10, 12):
                    sigmoid_gate(slot // 2 - 3)
                if 13 <= slot <= 16:
                    c_b = slot - 13
                    act.wait_ge(product_done, c_b + 1)
                    nc.scalar.activation(ah_t[:, c_b, :], tmp[0], ACT.Copy).then_inc(act_hi_ready, 1)
                if c is not None:
                    tap_products(c, first, end)
            hi(20)
            for c in range(4):
                act.wait_ge(a_normed, 3 * (c + 1))
                nc.scalar.activation(a_out[c], a_out[c], ACT.Silu, scale=cst("ln_a_g", c),
                                     bias=cst("ln_a_b", c)).then_inc(product_done, 1)
                act.wait_ge(product_done, 4 + c + 1)
                nc.scalar.activation(ah_t[:, c, 0:SEQ], a_out[c][:, 0:SEQ], ACT.Copy)
                nc.scalar.activation(ah_t[:, c, SAMPLE:SAMPLE + DEC], a_out[c][:, AO_SAMPLE:AO_SAMPLE + DEC],
                                     ACT.Copy).then_inc(act_hi_ready, 1)
            for s in range(4):
                hi(21 + s)
                for m in (2 * s, 2 * s + 1):
                    make_xg(1, m, JOB_DOWN_A + m)

            def last_down(p, job, slab):
                hi(slab + 1)
                for m in range(4):
                    make_xg(p + 1, m, job + m)
                hi(slab + 2)
                for m in range(4, 8):
                    make_xg(p + 1, m, job + m)

            def ffn(p):
                job, slab, a0, t0 = JOB0[p], SLAB0[p], ACT0[p], CONV0[p]
                for q in range(2):
                    hi(slab + 1 + 2 * q)
                    hi(slab + 2 + 2 * q)
                    silu_gate(t0 + q, q)
                    hidden_hi(a0 + q, q, q)
                with act.Fori(0, (FF_BLOCKS - 1) // 2) as i:
                    for b in range(2):
                        for step in range(6):
                            n = slab + 5 + 6 * b + step
                            split_hi(i * 12 + n, n % 2, i * 24 + AFTER[n - 2])
                            f = 2 * b + step // 2
                            if step in (1, 3):
                                silu_gate(i * 4 + (t0 + 2 + f), f % 2)
                            if step in (2, 4):
                                f = 2 * b + step // 2 - 1
                                hidden_hi(i * 4 + (a0 + 2 + f), f % 2, (2 + f) % 4)
                last_down(p, job + FF_JOBS - 8, slab + FF_SLABS - 2)

            ffn(1)
            for half in range(2):
                job, slab, a0 = JOB0[2] + 28 * half, SLAB0[2] + 16 * half, ACT0[2] + 4 * half
                for t in range(4):
                    hi(slab + 3 * t + 1)
                    hi(slab + 3 * t + 2)
                    hi(slab + 3 * t + 3)
                    hidden_hi(a0 + t, t % 2, t)
                hi(slab + 13)
                hi(slab + 14)
                if half == 0:
                    hi(slab + 15)
                    hi(slab + 16)
                else:
                    last_down(2, job + 20, slab + 14)
            ffn(3)

        @block.vector
        def _(dve):
            def tile3(pset):
                return psum[:, 3 * pset:3 * pset + 3, 0:CH]

            def cols3(ap):
                return ap.rearrange("p (c n) -> p c n", c=3)

            def times_r(job, pset, out):
                dve.wait_ge(tile_done, job + 1)
                dve.tensor_tensor(cols3(out), tile3(pset), r_3, ALU.mult).then_inc(tile_evacuated, 1)

            def sum_squares(p, m):
                dve.wait_ge(square_ready, KD * p + m + 1)
                if m >= 2:
                    dve.wait_ge(squares_summed, (KD - 1) * p + m - 1)
                dve.tensor_tensor(sumsq[:, 0:COLS], sumsq[:, 0:COLS], square[m % 2],
                                  ALU.add).then_inc(squares_summed, 1)

            def xg_low(p, m):
                dve.wait_ge(xg_hi_ready, KD * p + m + 1)
                dve.scalar_tensor_tensor(lo_t[:, m, :], x_t[:, m, :], cst("gain", p * KD + m),
                                         hi_t[:, m, :].bitcast(F32), ALU.mult,
                                         ALU.subtract).then_inc(xg_ready, 1)

            def clear_pad():
                dve.memset(sumsq[:, COLS:ROW_TILES * P], 0.0).then_inc(pad_cleared, 1)

            def add_down(job, pset, m, loaded=None):
                if loaded is not None:
                    dve.wait_ge(x_loaded[m], loaded)
                dve.wait_ge(tile_done, job + 1)
                dve.wait_ge(tile_evacuated, job)
                dve.tensor_tensor(cols3(x_t[:, m, :]), tile3(pset), cols3(x_t[:, m, :]),
                                  ALU.add).then_inc(tile_evacuated, 1)

            def last_down(p, job, pset):
                clear_pad()
                for m in range(KD):
                    add_down(job + m, (pset + m) % 2, m)
                    if m >= 1:
                        if p + 1 < 4:
                            xg_low(p + 1, m - 1)
                        if m >= 2:
                            sum_squares(p + 1, m - 1)
                if p + 1 < 4:
                    xg_low(p + 1, KD - 1)
                sum_squares(p + 1, KD - 1)

            def rms(p, tail):
                dve.wait_ge(stats_ready, p + 1)
                dve.tensor_scalar(mean_sq[:], psum[:, tail, CH + 2:CH + 2 + ROW_TILES], 1.0 / D, EPS, ALU.mult,
                                  ALU.add).then_inc(mean_sq_ready, 1)
                dve.wait_ge(r_spread, p + 1)
                dve.tensor_copy(r_rows[:, 0:1024], psum[:, 6:8, :].rearrange("p a b -> p (a b)")).then_inc(r_ready, 1)
                dve.tensor_copy(r_rows[:, 1024:COLS],
                                psum[:, tail, CH + 30:CH + 30 + COLS - 1024]).then_inc(r_ready, 1)
                dve.wait_ge(r_ready, 2 * (p + 1))

            def conv3(t, par, w_at, w_name, state_at, state_name, new, new_at):
                g = conv_in[par]
                last_frames = g[:, 992:1060].rearrange("p (a b) -> p a b", b=34)[:, :, 32:34]
                dve.tensor_scalar(new[:, bass.ds(new_at, 4)].rearrange("p (a b) -> p a b", a=2), last_frames,
                                  1.0, None, ALU.mult).then_inc(state_saved, 1)
                dve.tensor_scalar(g[:, SAMPLE:SAMPLE + 2], cst(state_name, state_at, 2), 1.0, None,
                                  ALU.mult).then_inc(history_set, 1)
                dve.wait_ge(history_set, t + 1)
                dve.tensor_scalar(conv_out[par], g[:, 0:COLS], cst(w_name, w_at), None,
                                  ALU.mult).then_inc(conv_tap, 1)
                for k in (1, 2):
                    dve.wait_ge(conv_tap, t * 3 + k)
                    dve.scalar_tensor_tensor(conv_out[par], g[:, k:k + COLS], cst(w_name, w_at + k), conv_out[par],
                                             ALU.mult, ALU.add).then_inc(conv_tap, 1)

            def hidden_lo(a, par, slot):
                dve.wait_ge(act_hi_ready, a + 1)
                dve.tensor_tensor(al_t[:, slot, :], prod[par], ah_t[:, slot, :].bitcast(F32),
                                  ALU.subtract).then_inc(act_ready, 1)

            dve.wait_ge(const_loaded, 16)
            clear_pad()
            for m in range(KD):
                xg_low(0, m)
                if m:
                    sum_squares(0, m)
            dve.memset(mv[:], 0.0).then_inc(pad_cleared, 1)
            dve.wait_ge(squares_summed, KD - 1)
            for c in range(4):
                dve.memset(a_in[c][:, 0:HA], 0.0).then_inc(glu_written, 1)
            rms(0, 0)

            taps_done = [0, 0, 0, 0]

            def taps(c, upto):
                for k in range(taps_done[c], min(upto, DVE_TAPS)):
                    w = cst("conv_a_w", c * TAPS_A + k)
                    src = a_in[c][:, k:k + AO_COLS]
                    if k == 0:
                        dve.wait_ge(glu_written, 4 * (c + 2))
                        if c:
                            dve.wait_ge(a_tap_product, POOL_TAPS * c)
                        dve.tensor_scalar(a_out[c], src, w, cst("conv_a_b", c), ALU.mult,
                                          ALU.add).then_inc(a_tap, 1)
                    else:
                        dve.wait_ge(a_tap, DVE_TAPS * c + k)
                        dve.scalar_tensor_tensor(a_out[c], src, w, a_out[c], ALU.mult, ALU.add).then_inc(a_tap, 1)
                taps_done[c] = upto
                if upto > DVE_TAPS:
                    dve.wait_ge(a_tap, DVE_TAPS * (c + 1))
                    dve.wait_ge(a_pool_sum, (POOL_TAPS - 1) * (c + 1))
                    dve.tensor_tensor(a_out[c], a_out[c], pool_sum, ALU.add).then_inc(a_conv_done, 1)

            def glu(c):
                a = a_in[c]
                dve.wait_ge(sigmoid_done, c + 1)
                dve.tensor_tensor(a[:, HA:HA + SEQ], tmp[0][:, 0:SEQ], tmp[1][:, 0:SEQ],
                                  ALU.mult).then_inc(glu_written, 1)
                dve.tensor_tensor(a[:, A_COLS - DEC:A_COLS], tmp[0][:, SAMPLE:SAMPLE + DEC],
                                  tmp[1][:, SAMPLE:SAMPLE + DEC], ALU.mult).then_inc(glu_written, 1)
                dve.tensor_copy(a[:, HA + SEQ:HA + SEQ + HA], cst("state_a", c * HA, HA)).then_inc(glu_written, 1)
                dve.wait_ge(glu_written, 4 + 4 * c + 3)
                last_frames = a[:, 992:A_COLS].rearrange("p (a b) -> p a b", b=62)[:, :, 32:62]
                dve.tensor_copy(new_a[:, c * 2 * HA:(c + 1) * 2 * HA].rearrange("p (a b) -> p a b", a=2),
                                last_frames).then_inc(glu_written, 1)

            def v_turned(c):
                job = JOB_VT[c]
                s = 3 * (job % 2)
                dve.wait_ge(tile_done, job + 1)
                dve.tensor_copy(v_rows[:, 0:8, c * P:(c + 1) * P],
                                psum[:, s:s + 2, :].rearrange("p a (b f) -> p (a b) f", f=P))
                dve.tensor_copy(v_rows[0:DEC, 8, c * P:(c + 1) * P],
                                psum[0:DEC, s + 2, 0:P]).then_inc(tile_evacuated, 1)

            def v_norm_stats():
                for t in range(ROW_TILES):
                    n = P if t < 8 else DEC
                    dve.bn_stats(bn[0:n, 6 * t:6 * t + 6], v_rows[0:n, t, :]).then_inc(row_stats, 1)
                for t in range(ROW_TILES):
                    n = P if t < 8 else DEC
                    dve.wait_ge(row_stats, t + 1)
                    dve.bn_aggr(mv[0:n, 2 * t:2 * t + 2], bn[0:n, 6 * t:6 * t + 6]).then_inc(row_moments, 1)
                dve.wait_ge(row_moments, ROW_TILES)
                dve.tensor_scalar(var_eps[:], mv[:].rearrange("p (t s) -> p t s", s=2)[:, :, 1], EPS, None,
                                  ALU.add).then_inc(var_ready, 1)

            def v_norm(first, end):
                dve.wait_ge(rstd_ready, 1)
                dve.wait_ge(mix_loaded, 48)
                for t in range(first, end):
                    n = P if t < 8 else DEC
                    v = v_rows[0:n, t, :]
                    dve.scalar_tensor_tensor(v, v, mv[0:n, 2 * t:2 * t + 1], lnv_g[0:n, :], ALU.subtract,
                                             ALU.mult).then_inc(v_scaled, 1)
                    dve.wait_ge(v_scaled, t + 1)
                    dve.scalar_tensor_tensor(v, v, rstd[0:n, t:t + 1], lnv_b[0:n, :], ALU.mult,
                                             ALU.add).then_inc(v_ready, 1)

            def mixed(c):
                job = JOB_S[c]
                s = 3 * (job % 2)
                dve.wait_ge(tile_done, job + 1)
                dve.tensor_tensor(tmp[1][:, 0:SEQ].rearrange("p (n i) -> p n i", i=P),
                                  psum[:, s:s + 2, :].rearrange("p a (b i) -> p (a b) i", i=P),
                                  mix_b[:, c:c + 1, :].to_broadcast([P, 8, P]), ALU.add)
                dve.tensor_tensor(tmp[1][:, SAMPLE:SAMPLE + DEC], psum[:, s + 2, 0:DEC], mix_b[:, c, 0:DEC],
                                  ALU.add).then_inc(tile_evacuated, 1)

            def gated_b(c):
                times_r(JOB_S[c] + 1, (JOB_S[c] + 1) % 2, tmp[0])
                dve.wait_ge(tile_evacuated, JOB_S[c] + 2)
                dve.tensor_tensor(tmp[0], tmp[0], tmp[1], ALU.mult).then_inc(product_done, 1)

            times_r(0, 0, tmp[0])
            times_r(1, 1, tmp[1])
            glu(0)
            taps(0, 3)
            times_r(2, 0, tmp[0])
            taps(0, 9)
            times_r(3, 1, tmp[1])
            glu(1)
            taps(0, 13)
            times_r(4, 0, tmp[0])
            taps(0, 18)
            times_r(5, 1, tmp[1])
            taps(0, DVE_TAPS + 1)
            v_turned(0)
            taps(1, 2)
            times_r(7, 1, tmp[0])
            taps(1, 5)
            v_turned(1)
            taps(1, 8)
            times_r(9, 1, tmp[1])
            dve.wait_ge(pad_cleared, 2)
            v_turned(2)
            v_turned(3)
            dve.wait_ge(tile_evacuated, 12)
            v_norm_stats()
            taps(1, 11)
            times_r(12, 0, tmp[0])
            dve.wait_ge(mix_loaded, 48)
            dve.memset(mix_w[64:P, :, 0:64], 0.0).then_inc(mask_set, 1)
            v_norm(0, 3)
            taps(1, 15)
            times_r(13, 1, tmp[1])
            glu(2)
            v_norm(3, 6)
            taps(1, 18)
            times_r(14, 0, tmp[0])
            v_norm(6, ROW_TILES)
            taps(1, DVE_TAPS + 1)
            taps(2, 2)
            times_r(15, 1, tmp[1])
            glu(3)
            taps(2, 4)
            for c in range(4):
                mixed(c)
                taps(2 if c < 3 else 3, [10, 16, DVE_TAPS + 1, 4][c])
                gated_b(c)
                dve.wait_ge(act_hi_ready, c + 1)
                dve.tensor_tensor(al_t[:, c, :], tmp[0], ah_t[:, c, :].bitcast(F32),
                                  ALU.subtract).then_inc(act_ready, 1)
            for m in range(KD):
                taps(3, min(4 + 3 * (m + 1), DVE_TAPS) if m < 6 else DVE_TAPS)
                if m == 6:
                    taps(3, DVE_TAPS + 1)
                    taps_done[3] = DVE_TAPS
                add_down(JOB_DOWN_B + m, m % 2, m, loaded=32)
            for t in range(ROW_TILES):
                n = P if t < 8 else DEC
                dve.wait_ge(a_rows_ready, t + 1)
                dve.bn_stats(bn[0:n, 6 * t:6 * t + 6], psum[0:n, 6 + t % 2, :]).then_inc(row_stats, 1)
                dve.wait_ge(row_stats, ROW_TILES + t + 1)
                dve.bn_aggr(mv[0:n, 2 * t:2 * t + 2], bn[0:n, 6 * t:6 * t + 6]).then_inc(row_moments, 1)
            dve.wait_ge(row_moments, 2 * ROW_TILES)
            mv_t = mv[:].rearrange("p (t s) -> p t s", s=2)
            dve.tensor_scalar(var_eps[:], mv_t[:, :, 1], EPS, None, ALU.add).then_inc(var_ready, 1)
            dve.wait_ge(rstd_ready, 2)
            dve.scalar_tensor_tensor(neg_mean[:], mv_t[:, :, 0], -1.0, rstd[:], ALU.mult,
                                     ALU.mult).then_inc(neg_mean_ready, 1)
            dve.wait_ge(tile_done, JOB_LN + 1)
            for c in range(4):
                o = a_out[c]
                s_cols = slice(AO_SAMPLE, AO_SAMPLE + DEC)
                for j in range(2):
                    dve.tensor_tensor(o[:, j * 512:(j + 1) * 512], o[:, j * 512:(j + 1) * 512], psum[:, 6 + j, :],
                                      ALU.mult).then_inc(a_scaled, 1)
                dve.tensor_tensor(o[:, s_cols], o[:, s_cols], psum[:, 2, 0:DEC], ALU.mult).then_inc(a_scaled, 1)
                dve.wait_ge(a_scaled, 3 * (c + 1))
                for j in range(2):
                    dve.tensor_tensor(o[:, j * 512:(j + 1) * 512], o[:, j * 512:(j + 1) * 512], psum[:, j, :],
                                      ALU.add).then_inc(a_normed, 1)
                dve.tensor_tensor(o[:, s_cols], o[:, s_cols], psum[:, 2, DEC:2 * DEC],
                                  ALU.add).then_inc(a_normed, 1)
            dve.wait_ge(a_normed, 12)
            dve.memset(bn[:, 0:1], 0.0).then_inc(tile_evacuated, 1)
            for c in range(4):
                dve.wait_ge(act_hi_ready, 4 + c + 1)
                dve.tensor_tensor(al_t[:, c, 0:SEQ], a_out[c][:, 0:SEQ], ah_t[:, c, 0:SEQ].bitcast(F32),
                                  ALU.subtract)
                dve.tensor_tensor(al_t[:, c, SAMPLE:SAMPLE + DEC], a_out[c][:, AO_SAMPLE:AO_SAMPLE + DEC],
                                  ah_t[:, c, SAMPLE:SAMPLE + DEC].bitcast(F32), ALU.subtract).then_inc(act_ready, 1)
            last_down(0, JOB_DOWN_A, 1)

            def clear_history():
                for g in conv_in:
                    dve.memset(g[:, 0:2], 0.0)

            def gate_tile(l, job, pset, t, f, par):
                times_r(job, pset, conv_in[par][:, 2:])
                dve.wait_ge(tile_evacuated, job + 1)
                at_f = f + l * FF_TILES
                conv3(t, par, at_f * 3, "conv_f_w", at_f * 2, "state_f", new_f, at_f * 4)

            def up_tile(job, pset, s, par):
                times_r(job, pset, prod[par])
                dve.wait_ge(tile_evacuated, job + 1)
                dve.wait_ge(silu_done, s + 1)
                dve.tensor_tensor(prod[par], prod[par], factor[par], ALU.mult).then_inc(product_done, 1)

            def ffn(p):
                l = (p - 1) // 2
                job, a0, t0 = JOB0[p], ACT0[p], CONV0[p]
                f0 = l * FF_TILES
                s0 = job % 2
                rms(p, 3 * s0)
                clear_history()
                gate_tile(l, job, s0, t0, 0, 0)
                up_tile(job + 1, 1 - s0, f0, 0)
                hidden_lo(a0, 0, 0)
                gate_tile(l, job + 2, s0, t0 + 1, 1, 1)
                up_tile(job + 3, 1 - s0, f0 + 1, 1)
                hidden_lo(a0 + 1, 1, 1)
                with dve.Fori(0, (FF_BLOCKS - 1) // 2) as i:
                    for b in range(2):
                        j = i * 24 + (job + 4 + 12 * b)
                        for q in range(2):
                            f = 2 + 2 * b + q
                            gate_tile(l, j + 2 * q, s0, i * 4 + (t0 + f), i * 4 + f, q)
                            up_tile(j + 2 * q + 1, 1 - s0, i * 4 + (f0 + f), q)
                            if q == 0:
                                hidden_lo(i * 4 + (a0 + f), q, f % 4)
                        add_down(j + 4, s0, 0)
                        hidden_lo(i * 4 + (a0 + 3 + 2 * b), 1, (3 + 2 * b) % 4)
                        for m in range(1, KD):
                            add_down(j + 4 + m, (s0 + m) % 2, m)
                last_down(p, job + FF_JOBS - 8, s0)

            ffn(1)
            p = 2
            s0 = JOB0[p] % 2
            rms(p, 3 * s0)
            clear_history()

            def c_tile(job, c):
                par = c % 2
                sets = [(job + q) % 2 for q in range(3)]
                times_r(job, sets[0], factor[par])
                times_r(job + 1, sets[1], prod[par])
                dve.wait_ge(tile_evacuated, job + 2)
                dve.tensor_tensor(conv_in[par][:, 2:], factor[par], prod[par], ALU.mult).then_inc(factor_ready, 1)
                dve.wait_ge(factor_ready, c + 1)
                conv3(CONV0[p] + c, par, c * 3, "conv_c_w", c * 2, "state_c", new_c, c * 4)
                times_r(job + 2, sets[2], prod[par])
                dve.wait_ge(tile_evacuated, job + 3)
                dve.wait_ge(conv_tap, 3 * (CONV0[p] + c + 1))
                dve.tensor_tensor(prod[par], prod[par], conv_out[par], ALU.mult).then_inc(product_done, 1)

            for half in range(2):
                job = JOB0[p] + 28 * half
                for t in range(4):
                    c = 4 * half + t
                    c_tile(job + 3 * t, c)
                    if t < 3:
                        hidden_lo(ACT0[p] + c, c % 2, t)
                for m in range(KD):
                    add_down(job + 12 + m, (s0 + m) % 2, m)
                    if m == 0:
                        hidden_lo(ACT0[p] + 4 * half + 3, 1, 3)
                if half == 0:
                    for m in range(KD):
                        add_down(job + 20 + m, (s0 + m) % 2, m)
                else:
                    last_down(p, job + 20, s0)
            ffn(3)
            rms(4, 0)
            for m in range(KD):
                dve.scalar_tensor_tensor(x_t[:, m, :], x_t[:, m, :], cst("gain", 4 * KD + m), r_rows[:],
                                         ALU.mult, ALU.mult).then_inc(y_ready, 1)


A_PLAN = [(2, 0, 0, 2), (3, 0, 2, 5), (4, 0, 5, 8), (5, 0, 8, 10), (6, 1, 0, 3), (7, 1, 3, 6), (8, 1, 6, 8),
          (9, 1, 8, 10), (10, 2, 0, 2), (11, 2, 2, 4), (12, 2, 4, 7), (13, 2, 7, 10), (14, 3, 0, 3),
          (15, 3, 3, 6), (16, 3, 6, 9), (17, 3, 9, 10), (18, None, 0, 0)]


def _pack(inputs):
    def cols(a):
        a = np.asarray(a)
        lead = a.reshape(-1, a.shape[-1] // P, P)
        return lead.transpose(2, 1, 0).reshape(P, -1)

    i = {k: np.asarray(v) for k, v in inputs.items()}
    xt = np.zeros((D, COLS), np.float32)
    xt[:, 0:SEQ] = i["x_prompt"][0].T
    xt[:, SAMPLE:SAMPLE + DEC] = i["x_sample"][0].T

    def up(w, t):
        return w[:, t * P:(t + 1) * P].reshape(KD, P, P).transpose(1, 0, 2).reshape(P, SLAB)

    def down(w, row, n_k, s):
        n_m = 8 // n_k
        part = w[row:row + n_k * P, s * n_m * P:(s + 1) * n_m * P]
        return part.reshape(n_k, P, n_m, P).transpose(1, 2, 0, 3).reshape(P, SLAB)

    slabs = []
    w, wo = i["w_in_ab"][0], i["w_out_ab"][0]
    order = [0, 4, 1, 5] + [12, 13, 14, 15] + [2, 6, 3, 7] + [8, 9, 10, 11]
    slabs += [up(w, t) for t in order]
    slabs += [down(wo, AW, 4, s) for s in range(4)] + [down(wo, 0, 4, s) for s in range(4)]

    def ffn(l):
        w, wd = i["w_up"][l], i["w_down"][l]
        for b in range(FF_BLOCKS):
            for f in (2 * b, 2 * b + 1):
                slabs.extend([up(w, f), up(w, FF_TILES + f)])
            if b:
                slabs.extend(down(wd, 2 * (b - 1) * P, 2, s) for s in range(2))
        slabs.extend(down(wd, 2 * (FF_BLOCKS - 1) * P, 2, s) for s in range(2))

    ffn(0)
    w, wo = i["w_in_c"][0], i["w_out_c"][0]
    for half in range(2):
        for c in range(4 * half, 4 * half + 4):
            slabs += [up(w, KD + c), up(w, 2 * KD + c), up(w, c)]
        for b in (2 * half, 2 * half + 1):
            slabs += [down(wo, 2 * b * P, 2, s) for s in range(2)]
    ffn(1)
    slabs = np.stack(slabs)
    assert slabs.shape[0] == N_SLABS

    gains = [i["norm_mix"][0], i["norm_ffn"][0], i["norm_mix"][1], i["norm_ffn"][1], i["norm_final"]]
    parts = {
        "gain": np.concatenate([cols(g) for g in gains], 1),
        "conv_a_w": cols(i["conv_a_w"][0]), "conv_a_b": cols(i["conv_a_b"][0]),
        "ln_a_g": cols(i["ln_a_g"][0]), "ln_a_b": cols(i["ln_a_b"][0]), "state_a": cols(i["state_conv_a"][0, 0]),
        "conv_c_w": cols(i["conv_c_w"][0]), "state_c": cols(i["state_conv_c"][0, 0]),
        "conv_f_w": np.concatenate([cols(i["conv_f_w"][l]) for l in range(2)], 1),
        "state_f": np.concatenate([cols(i["state_ffn"][l, 0]) for l in range(2)], 1),
    }
    consts = np.concatenate([parts[n] for n, _ in _SIZES], 1)
    assert consts.shape == (P, N_CONST)
    mix = i["ws_b"][0].transpose(2, 0, 1).reshape(P, 8 * P)
    bs = np.repeat(i["bs_b"][0].reshape(4, 2, P), 64, axis=1)
    bs = bs.transpose(1, 0, 2).reshape(P, 4 * P)
    lnv = np.tile(np.concatenate([i["ln_v_g"][0], i["ln_v_b"][0]])[None], (P, 1))
    return [("x_t", xt), ("slabs", slabs), ("consts", consts), ("mix", mix), ("bs", bs), ("lnv", lnv)]


_OUTS = [("y_t", (D, COLS)), ("a_state", (P, 4 * 2 * HA)), ("c_state", (P, KD * 4)),
         ("f_state", (P, 2 * FF_TILES * 4)), ("v_rows_out", (DEC, AW))]


def kernel(**inputs):
    import concourse.bacc as bacc
    from concourse.bass_utils import run_bass_kernel_spmd

    nc = bacc.Bacc("TRN2", target_bir_lowering=False, num_devices=1)
    arrays, args = {}, []
    for name, a in _pack(inputs):
        a = np.ascontiguousarray(a)
        arrays[name] = a
        args.append(nc.dram_tensor(name, a.shape, mybir.dt.from_np(a.dtype), kind="ExternalInput").ap())
    for name, shape in _OUTS:
        args.append(nc.dram_tensor(name, shape, F32, kind="ExternalOutput").ap())
    build(nc, *args)
    got = run_bass_kernel_spmd(nc, [arrays], core_ids=[0]).results[0]

    def rows(a, tiles, n):
        a = np.asarray(a).reshape(P, tiles, 2, n).transpose(2, 3, 1, 0).reshape(2, n, tiles * P)
        return a[0], a[1]

    y = np.asarray(got["y_t"])
    y_prompt = np.ascontiguousarray(y[:, 0:SEQ].T)[None]
    y_sample = np.ascontiguousarray(y[:, SAMPLE:SAMPLE + DEC].T)[None]
    a_p, a_s = rows(got["a_state"], 4, HA)
    c_p, c_s = rows(got["c_state"], KD, 2)
    f = np.asarray(got["f_state"]).reshape(P, 2, FF_TILES * 4)
    f_ps = [rows(np.ascontiguousarray(f[:, l]), FF_TILES, 2) for l in range(2)]
    f_p = np.stack([q[0][None] for q in f_ps])
    f_s = np.stack([q[1][None] for q in f_ps])
    v = np.asarray(got["v_rows_out"])[None, None]
    return (y_prompt, y_sample, a_p[None, None], a_s[None, None], c_p[None, None], c_s[None, None], f_p, f_s, v)
```

```python
import numpy as np

import concourse.bass as bass
from concourse import mybir
from contextlib import ExitStack

F32 = mybir.dt.float32
F32R = mybir.dt.float32r
ALU = mybir.AluOpType
ACT = mybir.ActivationFunctionType

P = 128
D = 1024
SEQ = 1024
DEC = 32
DFF = 2816
AW = 512
TAPS_A = 31
EPS = 1e-6

KD = D // P
SAMPLE = SEQ + 2
COLS = 1062
CH = COLS // 3
ROW_TILES = 9
FF_TILES = DFF // P
FF_BLOCKS = FF_TILES // 2
SLAB = 8 * P

HA = TAPS_A - 1
A_COLS = HA + SEQ + HA + DEC
AO_COLS = A_COLS - HA
AO_SAMPLE = SEQ + HA
POOL_TAPS = 10
DVE_TAPS = TAPS_A - POOL_TAPS

_SIZES = [("gain", 5 * KD), ("conv_a_w", 4 * TAPS_A), ("conv_a_b", 4), ("ln_a_g", 4), ("ln_a_b", 4),
          ("ln_v_g", 4), ("ln_v_b", 4), ("state_a", 4 * HA), ("conv_c_w", KD * 3), ("state_c", KD * 2),
          ("conv_f_w", 2 * FF_TILES * 3), ("state_f", 2 * FF_TILES * 2)]
OFF = {}
_at = 0
for _name, _size in _SIZES:
    OFF[_name] = _at
    _at += _size
N_CONST = _at

AB_SLABS = 24
JOB_A = [0, 2, 4, 14]
JOB_V = [6, 7, 9, 11]
JOB_VT = [8, 10, 12, 13]
JOB_S = [16, 18, 20, 22]
JOB_DOWN_B = 24
JOB_DOWN_A = 32
AB_JOBS = 40
ROWS_FROM = 2
SPREAD_STEP = 13
FF_SLABS = 6 * FF_BLOCKS
FF_JOBS = 12 * FF_BLOCKS
C_SLABS = 32
C_JOBS = 56

JOB0 = [0, AB_JOBS, AB_JOBS + FF_JOBS, AB_JOBS + FF_JOBS + C_JOBS]
SLAB0 = [0, AB_SLABS, AB_SLABS + FF_SLABS, AB_SLABS + FF_SLABS + C_SLABS]
N_SLABS = AB_SLABS + 2 * FF_SLABS + C_SLABS
N_JOBS = JOB0[3] + FF_JOBS


def _jobs_after_slab():
    after = []
    for c in (0, 1, 2):
        after += [JOB_A[c] + 1, JOB_A[c] + 2]
    after += [j + 1 for j in JOB_V]
    after += [JOB_A[3] + 1, JOB_A[3] + 2]
    after += [j + 2 for j in JOB_S]
    after += [JOB_DOWN_B + 2 * (s + 1) for s in range(4)]
    after += [JOB_DOWN_A + 2 * (s + 1) for s in range(4)]
    for phase in (1, 2, 3):
        at = JOB0[phase]
        if phase == 2:
            steps = ([1] * 12 + [4] * 4) * 2
        else:
            steps = [1] * 4 + ([1] * 4 + [4, 4]) * (FF_BLOCKS - 1) + [4, 4]
        for s in steps:
            at += s
            after.append(at)
    return after


AFTER = _jobs_after_slab()

def evacuated(job):
    return job + 1 if isinstance(job, int) and job < JOB_V[0] else job - 7


POOL_SUMS = 3
DVE_SUMS = KD - POOL_SUMS - 1


ACT0 = [0, 8, 8 + FF_TILES, 8 + FF_TILES + KD]
CONV0 = [None, 0, FF_TILES, FF_TILES + KD]


def build(nc, x_in, slabs, consts_in, mix_in, bs_in, lnv_in, y_out, a_state, c_state, f_state, v_out):
    with ExitStack() as ctx:
        def sb(name, cols, dt=F32):
            return ctx.enter_context(nc.sbuf_tensor(name, [P, cols], dt))

        def sem(name):
            return ctx.enter_context(nc.semaphore(name))

        x = sb("x", KD * COLS)
        xg_hi = sb("xg_hi", KD * COLS, F32R)
        xg_lo = sb("xg_lo", KD * COLS, F32R)
        act_hi = sb("act_hi", 4 * COLS, F32R)
        act_lo = sb("act_lo", 4 * COLS, F32R)
        raw = sb("raw", 2 * SLAB)
        w_hi = sb("w_hi", 2 * SLAB, F32R)
        w_lo = sb("w_lo", 2 * SLAB, F32R)
        r_rows = sb("r_rows", COLS)
        sumsq = sb("sumsq", ROW_TILES * P)
        work = sb("work", 4 * A_COLS + 2 * COLS + 2 * AO_COLS)
        const = sb("const", N_CONST)
        ident = sb("ident", P)
        ones = sb("ones", 64)
        minus_half = sb("minus_half", ROW_TILES)
        mean_sq = sb("mean_sq", ROW_TILES)
        mean_sq_s = sb("mean_sq_s", 1)
        r_col = sb("r_col", ROW_TILES)
        bn = sb("bn", ROW_TILES * 6)
        mv = sb("mv", ROW_TILES * 2)
        var_eps = sb("var_eps", ROW_TILES)
        rstd = sb("rstd", ROW_TILES)
        neg_mean = sb("neg_mean", ROW_TILES)
        conv_s = sb("conv_s", 4 * DEC)
        mix_bias = sb("mix_bias", P + DEC)
        new_a = sb("new_a", 4 * 2 * HA)
        new_c = sb("new_c", KD * 4)
        new_f = sb("new_f", 2 * FF_TILES * 4)
        psum = ctx.enter_context(nc.psum_tensor("psum", [P, 8, 512], F32))

        def cst(name, at, n=1):
            return const[:, bass.ds(OFF[name] + at, n)]

        x_t = x[:].rearrange("p (m n) -> p m n", m=KD)
        hi_t = xg_hi[:].rearrange("p (m n) -> p m n", m=KD)
        lo_t = xg_lo[:].rearrange("p (m n) -> p m n", m=KD)
        ah_t = act_hi[:].rearrange("p (m n) -> p m n", m=4)
        al_t = act_lo[:].rearrange("p (m n) -> p m n", m=4)
        r_3 = r_rows[:].rearrange("p (c n) -> p c n", c=3)

        GW = COLS + 2
        conv_in = [work[:, i * GW:(i + 1) * GW] for i in range(2)]
        conv_out = [work[:, (2 + i) * GW:(2 + i) * GW + COLS] for i in range(2)]
        factor = [work[:, (4 + i) * GW:(4 + i) * GW + COLS] for i in range(2)]
        prod = [work[:, (6 + i) * GW:(6 + i) * GW + COLS] for i in range(2)]
        a_in = [work[:, c * A_COLS:(c + 1) * A_COLS] for c in range(4)]
        a_out = [work[:, c * A_COLS:c * A_COLS + AO_COLS] for c in range(4)]
        tmp = [work[:, 4 * A_COLS + i * COLS:4 * A_COLS + (i + 1) * COLS] for i in range(2)]
        at = 4 * A_COLS + 2 * COLS
        tap_prod = [sumsq[:, 0:AO_COLS], work[:, at:at + AO_COLS]]
        conv_acc = psum[:, 6:8, :].rearrange("p a b -> p (a b)")
        square = [work[:, m * COLS:(m + 1) * COLS] for m in range(KD)]
        v_rows = x[:, 0:ROW_TILES * AW].rearrange("p (t f) -> p t f", t=ROW_TILES)
        at = ROW_TILES * AW
        mix_w = x[:, at:at + 8 * P].rearrange("p (g i) -> p g i", g=8)
        at += 8 * P
        mix_b = x[:, at:at + 4 * P].rearrange("p (c i) -> p c i", c=4)
        at += 4 * P
        lnv_g = x[0:DEC, at:at + AW]
        lnv_b = x[0:DEC, at + AW:at + 2 * AW]
        lnv = x[0:DEC, at:at + 2 * AW]
        assert at + 2 * AW <= KD * COLS - AO_COLS
        pool_sum = [x[:, KD * COLS - AO_COLS:KD * COLS], work[:, 4 * A_COLS + 2 * COLS + AO_COLS:]]

        const_loaded = sem("const_loaded")
        x_loaded = [sem(f"x_loaded{m}") for m in range(KD)]
        mix_loaded = sem("mix_loaded")
        raw_loaded = [sem(f"raw_loaded{i}") for i in range(2)]
        weights_hi = sem("weights_hi")
        weights_ready = sem("weights_ready")
        consts_made = sem("consts_made")
        pad_cleared = sem("pad_cleared")
        tile_done = sem("tile_done")
        tile_evacuated = sem("tile_evacuated")
        xg_hi_ready = sem("xg_hi_ready")
        xg_ready = sem("xg_ready")
        square_ready = sem("square_ready")
        squares_summed = sem("squares_summed")
        stats_ready = sem("stats_ready")
        mean_sq_ready = sem("mean_sq_ready")
        r_col_ready = sem("r_col_ready")
        r_spread = sem("r_spread")
        r_ready = sem("r_ready")
        state_saved = sem("state_saved")
        history_set = sem("history_set")
        conv_tap = sem("conv_tap")
        factor_ready = sem("factor_ready")
        product_done = sem("product_done")
        act_hi_ready = sem("act_hi_ready")
        act_ready = sem("act_ready")
        sigmoid_done = sem("sigmoid_done")
        glu_written = sem("glu_written")
        a_tap = sem("a_tap")
        a_tap_product = sem("a_tap_product")
        a_pool_sum = sem("a_pool_sum")
        a_conv_done = sem("a_conv_done")
        a_acc_s = sem("a_acc_s")
        early_sum = sem("early_sum")
        v_evacuated = sem("v_evacuated")
        mix_bias_ready = sem("mix_bias_ready")
        mix_times_r = sem("mix_times_r")
        ln_spread = sem("ln_spread")
        ln_copied = sem("ln_copied")
        x_scaled = sem("x_scaled")
        y_ready_pool = sem("y_ready_pool")
        a_rows_ready = sem("a_rows_ready")
        row_stats = sem("row_stats")
        row_moments = sem("row_moments")
        var_ready = sem("var_ready")
        rstd_ready = sem("rstd_ready")
        neg_mean_ready = sem("neg_mean_ready")
        v_ready = sem("v_ready")
        v_sample_ready = sem("v_sample_ready")
        mask_set = sem("mask_set")
        a_scaled = sem("a_scaled")
        a_normed = sem("a_normed")
        a_silu_done = sem("a_silu_done")
        silu_done = sem("silu_done")
        y_ready = sem("y_ready")
        v_stored = sem("v_stored")
        stored = sem("stored")

        block = ctx.enter_context(nc.Block())

        @block.sync
        def _(sp):
            def load_slab(n, slot):
                sp.dma_start(raw[:, slot * SLAB:(slot + 1) * SLAB],
                             slabs[bass.ds(n, 1), :, :].rearrange("s p n -> p (s n)")).then_inc(raw_loaded[slot], 16)

            def load_slabs(first, end):
                for n in range(first, end):
                    sp.wait_ge(weights_ready, n - 1)
                    load_slab(n, n % 2)

            def load_x(m):
                sp.dma_start(x_t[:, m, :], x_in[m * P:(m + 1) * P, :]).then_inc(x_loaded[m], 16)

            load_slab(0, 0)
            sp.dma_start(const[:], consts_in).then_inc(const_loaded, 16)
            for m in range(KD):
                load_x(m)
                if m == 2:
                    load_slab(1, 1)
            load_slabs(2, 4)
            sp.wait_ge(xg_ready, KD)
            sp.wait_ge(squares_summed, DVE_SUMS)
            sp.dma_start(mix_w, mix_in.rearrange("p (g i) -> p g i", g=8)).then_inc(mix_loaded, 16)
            sp.dma_start(mix_b, bs_in.rearrange("p (c i) -> p c i", c=4)).then_inc(mix_loaded, 16)
            sp.dma_start(lnv, lnv_in).then_inc(mix_loaded, 16)
            load_slabs(4, 14)
            sp.wait_ge(v_sample_ready, 2)
            sp.dma_start(v_out, lnv_g).then_inc(v_stored, 16)
            load_slabs(14, 18)
            sp.wait_ge(tile_evacuated, evacuated(JOB_S[3]))
            sp.wait_ge(v_stored, 16)
            sp.wait_ge(a_conv_done, 6)
            load_x(0)
            load_x(1)
            load_slabs(18, 19)
            load_x(2)
            load_x(3)
            load_slabs(19, 20)
            load_x(4)
            load_x(5)
            load_slabs(20, 21)
            load_x(6)
            load_x(7)
            load_slabs(21, 22)
            sp.wait_ge(glu_written, 20)
            sp.dma_start(a_state, new_a[:]).then_inc(stored, 16)
            with sp.Fori(11, N_SLABS // 2) as i:
                sp.wait_ge(weights_ready, i * 2 - 1)
                load_slab(i * 2, 0)
                sp.wait_ge(weights_ready, i * 2)
                load_slab(i * 2 + 1, 1)
            sp.wait_ge(state_saved, 2 * FF_TILES + KD)
            sp.dma_start(c_state, new_c[:]).then_inc(stored, 16)
            sp.dma_start(f_state, new_f[:]).then_inc(stored, 16)
            for m in range(KD):
                if m in POOL_Y:
                    sp.wait_ge(y_ready_pool, POOL_Y.index(m) + 1)
                else:
                    sp.wait_ge(y_ready, m + 1 - sum(q < m for q in POOL_Y))
                sp.dma_start(y_out[m * P:(m + 1) * P, :], x_t[:, m, :]).then_inc(stored, 16)
            sp.wait_ge(stored, 16 * (3 + KD))

        @block.tensor
        def _(pe):
            def split_product(out, w_at, slot, hi, lo, start, stop):
                s = slice(slot * SLAB + w_at * P, slot * SLAB + (w_at + 1) * P)
                nc.tensor.matmul(out, w_hi[:, s], hi, start=start, stop=False)
                nc.tensor.matmul(out, w_hi[:, s], lo, start=False, stop=False)
                return nc.tensor.matmul(out, w_lo[:, s], hi, start=False, stop=stop)

            def bank(pset, c):
                return psum[:, 3 * pset + c, 0:CH]

            def up_part(pset, slot, ks):
                last = None
                for k in ks:
                    for c in range(3):
                        cols = slice(c * CH, (c + 1) * CH)
                        last = split_product(bank(pset, c), k, slot, hi_t[:, k, cols], lo_t[:, k, cols],
                                             k == 0, k == KD - 1)
                return last

            def banks_free(job):
                if isinstance(job, int) and JOB_V[0] <= job - 2 <= JOB_VT[3]:
                    pe.wait_ge(v_evacuated, job - 2 - JOB_V[0] + 1)
                elif not isinstance(job, int) or job >= 2:
                    pe.wait_ge(tile_evacuated, evacuated(job - 2))

            def up_job(job, slab, pset, slot, fresh=None):
                banks_free(job)
                pe.wait_ge(weights_ready, slab + 1)
                if fresh is None:
                    up_part(pset, slot, range(KD)).then_inc(tile_done, 1)
                else:
                    for k in range(KD):
                        pe.wait_ge(xg_ready, KD * fresh + k + 1)
                        last = up_part(pset, slot, [k])
                    last.then_inc(tile_done, 1)

            def down_jobs(job, slab, acts, act0, n_k, pset, slot, between=None):
                pe.wait_ge(weights_ready, slab + 1)
                for m in range(8 // n_k):
                    banks_free(job + m)
                    for k in range(n_k):
                        if between is not None:
                            between(m, k)
                        if acts is not None and m == 0:
                            pe.wait_ge(act_ready, acts + k + 1)
                        for c in range(3):
                            cols = slice(c * CH, (c + 1) * CH)
                            last = split_product(bank((pset + m) % 2, c), m * n_k + k, slot,
                                                 ah_t[:, act0 + k, cols], al_t[:, act0 + k, cols],
                                                 k == 0, k == n_k - 1)
                    last.then_inc(tile_done, 1)

            def rms_stats(p, tail):
                pe.wait_ge(squares_summed, DVE_SUMS * (p + 1))
                if p == 0:
                    nc.tensor.matmul(psum[0:DEC, tail, CH + 20:CH + 21], sumsq[:, SAMPLE:SAMPLE + DEC],
                                     ones[:, 0:1], start=True, stop=True)
                for t in range(ROW_TILES):
                    last = nc.tensor.matmul(psum[:, tail, CH + 2 + t:CH + 3 + t], sumsq[:, t * P:(t + 1) * P],
                                            ones[:, 0:1], start=True, stop=True)
                last.then_inc(stats_ready, 1)

            def rms_spread(p, tail):
                pe.wait_ge(r_col_ready, p + 1)
                for t in range(ROW_TILES):
                    n = min(P, COLS - t * P)
                    out = psum[:, 6 + t // 4, (t % 4) * P:(t % 4 + 1) * P] if t < 8 else \
                        psum[:, tail, CH + 30:CH + 30 + n]
                    last = nc.tensor.matmul(out, r_col[:, t:t + 1].to_broadcast([P, P]), ident[:, 0:n],
                                            start=True, stop=True)
                last.then_inc(r_spread, 1)

            def phase_start(p):
                job, slab = JOB0[p], SLAB0[p]
                a, b = job % 2, (job + 1) % 2
                early, late = (4, 7) if p == 0 else (0, 5)
                up_job(job, slab, a, slab % 2, fresh=p)
                banks_free(job + 1)
                pe.wait_ge(weights_ready, slab + 2)
                up_part(b, (slab + 1) % 2, range(0, early))
                rms_stats(p, 3 * a)
                up_part(b, (slab + 1) % 2, range(early, late))
                rms_spread(p, 3 * a)
                up_part(b, (slab + 1) % 2, range(late, KD)).then_inc(tile_done, 1)

            def turn_v(c):
                job = JOB_VT[c]
                s = 3 * (job % 2)
                pe.wait_ge(v_evacuated, JOB_V[c] - JOB_V[0] + 1)
                banks_free(job)
                for t in range(8):
                    nc.tensor.transpose(psum[:, s + t // 4, (t % 4) * P:(t % 4 + 1) * P],
                                        tmp[c % 2][:, t * P:(t + 1) * P], ident[:])
                nc.tensor.transpose(psum[0:DEC, s + 2, 0:P], tmp[c % 2][:, SAMPLE:SAMPLE + DEC],
                                    ident[:]).then_inc(tile_done, 1)

            def mix(c):
                job = JOB_S[c]
                s = 3 * (job % 2)
                banks_free(job)
                for h in range(2):
                    g = 2 * c + h
                    rows = slice(64 * h, 64 * h + 64)
                    for n in range(8):
                        nc.tensor.matmul(psum[rows, s + n // 4, (n % 4) * P:(n % 4 + 1) * P],
                                         v_rows[:, n, 64 * g:64 * g + 64], mix_w[:, g, :],
                                         start=True, stop=True)
                    nc.tensor.matmul(psum[rows, s + 2, DEC:DEC + P], ones[:], mix_w[:, g, :],
                                     start=True, stop=True)
                    nc.tensor.matmul(psum[rows, s + 2, 0:DEC], v_rows[0:DEC, 8, 64 * g:64 * g + 64],
                                     mix_w[0:DEC, g, 0:DEC], start=True, stop=True)
                    last = nc.tensor.matmul(psum[rows, s + 2, DEC + P:2 * DEC + P], ones[0:DEC, :],
                                            mix_w[0:DEC, g, 0:DEC], start=True, stop=True)
                last.then_inc(tile_done, 1)

            def a_rows(t):
                if t == 0:
                    pe.wait_ge(a_conv_done, 8)
                if t >= 2:
                    pe.wait_ge(row_stats, ROW_TILES + t - 1)
                n = P if t < 8 else DEC
                at_col = t * P if t < 8 else AO_SAMPLE
                for c in range(4):
                    last = nc.tensor.transpose(psum[0:n, 6 + t % 2, c * P:(c + 1) * P],
                                               a_out[c][:, at_col:at_col + n], ident[:])
                last.then_inc(a_rows_ready, 1)

            def spread_ln(n, col, job):
                b0 = 3 * ((job - 1) % 2)
                pe.wait_ge(tile_evacuated, evacuated(job - 1))
                if n == 0:
                    pe.wait_ge(neg_mean_ready, 2)
                    pe.wait_ge(row_stats, 2 * ROW_TILES)
                else:
                    pe.wait_ge(ln_copied, 1)
                for t in range(ROW_TILES):
                    k = P if t < 8 else DEC
                    out = psum[:, 6 + t // 4, (t % 4) * P:(t % 4 + 1) * P] if t < 8 else \
                        psum[:, b0, CH + 2:CH + 2 + DEC]
                    last = nc.tensor.matmul(out, col[0:k, t:t + 1].to_broadcast([k, P]), ident[0:k, 0:k],
                                            start=True, stop=True)
                last.then_inc(ln_spread, 1)

            def a_statistics(first):
                def between(m, k):
                    step = 4 * (first + m - ROWS_FROM) + k
                    if 0 <= step < ROW_TILES:
                        a_rows(step)
                    for n, col in enumerate((rstd, neg_mean)):
                        if step == SPREAD_STEP + 4 * n:
                            spread_ln(n, col, JOB_DOWN_B + first + m)
                        if step == SPREAD_STEP + 4 * n + 3:
                            pe.wait_ge(ln_copied, n + 1)
                return between

            pe.wait_ge(consts_made, 4)
            phase_start(0)
            for q in range(4):
                up_job(2 + q, 2 + q, q % 2, q % 2)
            up_job(6, 6, 0, 0)
            up_job(7, 7, 1, 1)
            turn_v(0)
            up_job(9, 8, 1, 0)
            turn_v(1)
            up_job(11, 9, 1, 1)
            turn_v(2)
            turn_v(3)
            up_job(14, 10, 0, 0)
            up_job(15, 11, 1, 1)
            pe.wait_ge(v_ready, ROW_TILES)
            pe.wait_ge(mask_set, 1)
            for c in range(4):
                mix(c)
                up_job(JOB_S[c] + 1, 12 + c, 1, c % 2)
            for s in range(4):
                down_jobs(JOB_DOWN_B + 2 * s, 16 + s, 0 if s == 0 else None, 0, 4, 0, s % 2,
                          between=a_statistics(2 * s))
            for s in range(4):
                down_jobs(JOB_DOWN_A + 2 * s, 20 + s, 4 if s == 0 else None, 0, 4, 0, s % 2)

            def ffn(p):
                job, slab, act = JOB0[p], SLAB0[p], ACT0[p]
                s0 = job % 2
                phase_start(p)
                up_job(job + 2, slab + 2, s0, 0)
                up_job(job + 3, slab + 3, 1 - s0, 1)
                with pe.Fori(0, (FF_BLOCKS - 1) // 2) as i:
                    for q in range(2):
                        j = i * 24 + (job + 4 + 12 * q)
                        s = i * 12 + (slab + 4 + 6 * q)
                        for t in range(4):
                            up_job(j + t, s + t, (s0 + t) % 2, t % 2)
                        down_jobs(j + 4, s + 4, i * 4 + (act + 2 * q), 2 * q, 2, s0, 0)
                        down_jobs(j + 8, s + 5, None, 2 * q, 2, s0, 1)
                j, s = job + FF_JOBS - 8, slab + FF_SLABS - 2
                down_jobs(j, s, act + FF_TILES - 2, 0, 2, s0, 0)
                down_jobs(j + 4, s + 1, None, 0, 2, s0, 1)

            ffn(1)
            s0 = JOB0[2] % 2
            for half in range(2):
                job, slab = JOB0[2] + 28 * half, SLAB0[2] + 16 * half
                if half == 0:
                    phase_start(2)
                for t in range(0 if half else 2, 12):
                    up_job(job + t, slab + t, (s0 + t) % 2, t % 2)
                for q in range(2):
                    down_jobs(job + 12 + 8 * q, slab + 12 + 2 * q, ACT0[2] + 4 * half + 2 * q, 2 * q, 2, s0, 0)
                    down_jobs(job + 16 + 8 * q, slab + 13 + 2 * q, None, 2 * q, 2, s0, 1)
            ffn(3)
            rms_stats(4, 0)
            rms_spread(4, 0)

        @block.gpsimd
        def _(pool):
            nc.gpsimd.memset(ident[:], 0.0).then_inc(consts_made, 1)
            nc.gpsimd.memset(minus_half[:], -0.5).then_inc(consts_made, 1)
            nc.gpsimd.memset(ones[:], 1.0).then_inc(consts_made, 1)
            pool.wait_ge(consts_made, 3)
            nc.gpsimd.affine_select(out=ident[:], in_=ident[:], compare_op=ALU.not_equal, fill=1.0, base=0,
                                    pattern=[[-1, P]], channel_multiplier=1).then_inc(consts_made, 1)

            def split_lo(n, slot):
                pool.wait_ge(weights_hi, n + 1)
                s = slice(slot * SLAB, (slot + 1) * SLAB)
                nc.gpsimd.tensor_tensor(w_lo[:, s], raw[:, s], w_hi[:, s].bitcast(F32),
                                        ALU.subtract).then_inc(weights_ready, 1)

            def early_squares(p, m):
                pool.wait_ge(square_ready, KD * p + m + 1)
                if m > 1:
                    pool.wait_ge(early_sum, POOL_SUMS * p + m - 1)
                nc.gpsimd.tensor_tensor(sumsq[:, 0:COLS], square[0] if m == 1 else sumsq[:, 0:COLS],
                                        square[m], ALU.add).then_inc(early_sum, 1)

            def r_of_frames(p):
                pool.wait_ge(mean_sq_ready, p + 1)
                nc.gpsimd.tensor_tensor(r_col[:], mean_sq[:], minus_half[:], ALU.pow).then_inc(r_col_ready, 1)

            def pool_taps(c, first, end):
                for i in range(first, end):
                    if i == 0:
                        continue
                    pool.wait_ge(a_tap_product, POOL_TAPS * c + i + 1)
                    if i == 1:
                        if c >= 2:
                            pool.wait_ge(a_conv_done, 2 * (c - 1))
                        a = tap_prod[(POOL_TAPS * c) % 2]
                    else:
                        pool.wait_ge(a_pool_sum, (POOL_TAPS - 1) * c + i - 1)
                        a = pool_sum[c % 2]
                    nc.gpsimd.tensor_tensor(pool_sum[c % 2], a, tap_prod[(POOL_TAPS * c + i) % 2],
                                            ALU.add).then_inc(a_pool_sum, 1)

            def row_rstd(n):
                pool.wait_ge(var_ready, n)
                nc.gpsimd.tensor_tensor(rstd[:], var_eps[:], minus_half[:], ALU.pow).then_inc(rstd_ready, 1)

            split_lo(0, 0)
            split_lo(1, 1)
            for m in (1, 2, 3):
                early_squares(0, m)
            r_of_frames(0)
            split_lo(2, 0)
            for slot in range(2, 19):
                split_lo(slot + 1, (slot + 1) % 2)
                for c, first, end in A_PLAN.get(slot, ()):
                    pool_taps(c, first, end)
                if slot == 10:
                    row_rstd(1)
                if slot == 16 + (ROWS_FROM + 2) // 2:
                    row_rstd(2)
            split_lo(20, 0)
            split_lo(21, 1)
            early_squares(1, 1)
            split_lo(22, 0)
            early_squares(1, 2)
            early_squares(1, 3)
            split_lo(23, 1)
            for p in (1, 2, 3):
                n0 = SLAB0[p]
                n1 = SLAB0[p + 1] if p < 3 else N_SLABS
                split_lo(n0, 0)
                split_lo(n0 + 1, 1)
                r_of_frames(p)
                with pool.Fori(1, (n1 - n0) // 2) as i:
                    split_lo(i * 2 + n0, 0)
                    split_lo(i * 2 + n0 + 1, 1)
                for m in (1, 2, 3):
                    early_squares(p + 1, m)
            r_of_frames(4)
            for n, m in enumerate(POOL_Y):
                pool.wait_ge(x_scaled, n + 1)
                pool.wait_ge(r_ready, 10)
                nc.gpsimd.tensor_tensor(x_t[:, m, :], x_t[:, m, :], r_rows[:], ALU.mult).then_inc(y_ready_pool, 1)

        @block.scalar
        def _(act):
            def split_hi(n, slot, after):
                act.wait_ge(raw_loaded[slot], n * 8 + (16 - 8 * slot))
                if after is not None:
                    act.wait_ge(tile_done, after)
                s = slice(slot * SLAB, (slot + 1) * SLAB)
                nc.scalar.activation(w_hi[:, s], raw[:, s], ACT.Copy).then_inc(weights_hi, 1)

            def hi(n):
                if n < N_SLABS:
                    split_hi(n, n % 2, AFTER[n - 2] if n >= 2 else None)

            def xg_high(p, m):
                nc.scalar.activation(hi_t[:, m, :], x_t[:, m, :], ACT.Identity,
                                     scale=cst("gain", p * KD + m)).then_inc(xg_hi_ready, 1)

            def make_xg(p, m, job):
                act.wait_ge(tile_evacuated, evacuated(job))
                if p < 4:
                    xg_high(p, m)
                nc.scalar.activation(square[m], x_t[:, m, :], ACT.Square).then_inc(square_ready, 1)
                if p == 4 and m in POOL_Y:
                    act.wait_ge(square_ready, KD * p + m + 1)
                    nc.scalar.activation(x_t[:, m, :], x_t[:, m, :], ACT.Identity,
                                         scale=cst("gain", p * KD + m)).then_inc(x_scaled, 1)

            def hidden_hi(a, par, slot):
                act.wait_ge(product_done, a - ACT0[1] + 1)
                nc.scalar.activation(ah_t[:, slot, :], prod[par], ACT.Copy).then_inc(act_hi_ready, 1)

            def silu_gate(t, par):
                act.wait_ge(conv_tap, t * 3 + 3)
                nc.scalar.activation(factor[par], conv_out[par], ACT.Silu).then_inc(silu_done, 1)

            def tap_products(c, first, end):
                for i in range(first, end):
                    if i == 0:
                        act.wait_ge(glu_written, 4 * (c + 2))
                    n = POOL_TAPS - 1
                    used = n * c - 1 if i == 0 else n * c if i == 1 else n * c + max(1, i - 2)
                    if used > 0:
                        act.wait_ge(a_pool_sum, used)
                    k = DVE_TAPS + i
                    nc.scalar.activation(tap_prod[(POOL_TAPS * c + i) % 2], a_in[c][:, k:k + AO_COLS], ACT.Identity,
                                         scale=cst("conv_a_w", c * TAPS_A + k)).then_inc(a_tap_product, 1)

            def sigmoid_gate(c):
                act.wait_ge(tile_evacuated, evacuated(JOB_A[c] + 1))
                nc.scalar.activation(tmp[1], tmp[1], ACT.Sigmoid).then_inc(sigmoid_done, 1)

            def first_squares(*tiles):
                for m in tiles:
                    nc.scalar.activation(square[m], x_t[:, m, :], ACT.Square).then_inc(square_ready, 1)

            hi(0)
            act.wait_ge(const_loaded, 16)
            for m in range(KD):
                act.wait_ge(x_loaded[m], 16)
                xg_high(0, m)
                if m == 0:
                    first_squares(0)
                if m == 2:
                    first_squares(1)
                    hi(1)
                if m == 3:
                    first_squares(2)
            first_squares(*range(3, KD))
            hi(2)

            def v_out_of_psum(c):
                job = JOB_V[c]
                act.wait_ge(tile_done, job + 1)
                if c == 0:
                    act.wait_ge(glu_written, 16)
                if c >= 2:
                    act.wait_ge(tile_done, JOB_VT[c - 2] + 1)
                nc.scalar.activation(tmp[c % 2].rearrange("p (c n) -> p c n", c=3),
                                     psum[:, 3 * (job % 2):3 * (job % 2) + 3, 0:CH],
                                     ACT.Copy).then_inc(v_evacuated, 1)

            def v_rows_out_of_psum(c):
                job = JOB_VT[c]
                s = 3 * (job % 2)
                act.wait_ge(tile_done, job + 1)
                nc.scalar.activation(v_rows[:, 0:8, c * P:(c + 1) * P],
                                     psum[:, s:s + 2, :].rearrange("p a (b f) -> p (a b) f", f=P), ACT.Copy)
                nc.scalar.activation(v_rows[0:DEC, 8, c * P:(c + 1) * P], psum[0:DEC, s + 2, 0:P],
                                     ACT.Copy).then_inc(v_evacuated, 1)

            def v_norm():
                act.wait_ge(neg_mean_ready, 1)
                for t in reversed(range(ROW_TILES)):
                    n = P if t < 8 else DEC
                    nc.scalar.activation(v_rows[0:n, t, :], v_rows[0:n, t, :], ACT.Identity,
                                         scale=rstd[0:n, t:t + 1],
                                         bias=neg_mean[0:n, t:t + 1]).then_inc(v_ready, 1)

            def b_hi(c):
                act.wait_ge(tile_evacuated, evacuated(JOB_S[c] + 1))
                nc.scalar.activation(ah_t[:, c, :], tmp[0], ACT.Copy).then_inc(act_hi_ready, 1)

            for slot in range(2, 19):
                if slot in (7, 8, 9, 10):
                    v_out_of_psum(slot - 7)
                if slot == 10:
                    v_rows_out_of_psum(2)
                hi(slot + 1)
                if slot in (2, 4, 6):
                    sigmoid_gate(slot // 2 - 1)
                if slot in (8, 9):
                    v_rows_out_of_psum(slot - 8)
                if slot == 10:
                    v_rows_out_of_psum(3)
                if slot == 12:
                    sigmoid_gate(3)
                if slot in (13, 14, 15, 16):
                    b_hi(slot - 13)
                for c, first, end in A_PLAN.get(slot, ()):
                    tap_products(c, first, end)
                if slot == 10:
                    v_norm()

            def ln_out_of_psum(n, b0):
                dst = tap_prod[n]
                act.wait_ge(ln_spread, n + 1)
                nc.scalar.activation(dst[:, 0:SEQ], psum[:, 6:8, :].rearrange("p a b -> p (a b)"), ACT.Copy)
                nc.scalar.activation(dst[:, AO_SAMPLE:AO_SAMPLE + DEC], psum[:, b0, CH + 2:CH + 2 + DEC],
                                     ACT.Copy).then_inc(ln_copied, 1)

            ln_out_of_psum(0, 0)
            hi(20)
            ln_out_of_psum(1, 3)
            for c in range(4):
                act.wait_ge(a_normed, c + 1)
                nc.scalar.activation(a_out[c], a_out[c], ACT.Silu, scale=cst("ln_a_g", c),
                                     bias=cst("ln_a_b", c)).then_inc(a_silu_done, 1)
            act.wait_ge(tile_done, JOB_DOWN_A)
            for c in range(4):
                act.wait_ge(a_silu_done, c + 1)
                nc.scalar.activation(ah_t[:, c, 0:SEQ], a_out[c][:, 0:SEQ], ACT.Copy)
                nc.scalar.activation(ah_t[:, c, SAMPLE:SAMPLE + DEC], a_out[c][:, AO_SAMPLE:AO_SAMPLE + DEC],
                                     ACT.Copy).then_inc(act_hi_ready, 1)
            for s in range(4):
                hi(21 + s)
                for m in (2 * s, 2 * s + 1):
                    make_xg(1, m, JOB_DOWN_A + m)

            def last_down(p, job, slab):
                hi(slab + 1)
                for m in range(4):
                    make_xg(p + 1, m, job + m)
                hi(slab + 2)
                for m in range(4, 8):
                    make_xg(p + 1, m, job + m)

            def ffn(p):
                job, slab, a0, t0 = JOB0[p], SLAB0[p], ACT0[p], CONV0[p]
                for q in range(2):
                    hi(slab + 1 + 2 * q)
                    hi(slab + 2 + 2 * q)
                    silu_gate(t0 + q, q)
                    hidden_hi(a0 + q, q, q)
                with act.Fori(0, (FF_BLOCKS - 1) // 2) as i:
                    for b in range(2):
                        for step in range(6):
                            n = slab + 5 + 6 * b + step
                            split_hi(i * 12 + n, n % 2, i * 24 + AFTER[n - 2])
                            f = 2 * b + step // 2
                            if step in (1, 3):
                                silu_gate(i * 4 + (t0 + 2 + f), f % 2)
                            if step in (2, 4):
                                f = 2 * b + step // 2 - 1
                                hidden_hi(i * 4 + (a0 + 2 + f), f % 2, (2 + f) % 4)
                last_down(p, job + FF_JOBS - 8, slab + FF_SLABS - 2)

            ffn(1)
            for half in range(2):
                job, slab, a0 = JOB0[2] + 28 * half, SLAB0[2] + 16 * half, ACT0[2] + 4 * half
                for t in range(4):
                    hi(slab + 3 * t + 1)
                    hi(slab + 3 * t + 2)
                    hi(slab + 3 * t + 3)
                    hidden_hi(a0 + t, t % 2, t)
                hi(slab + 13)
                hi(slab + 14)
                if half == 0:
                    hi(slab + 15)
                    hi(slab + 16)
                else:
                    last_down(2, job + 20, slab + 14)
            ffn(3)

        @block.vector
        def _(dve):
            def tile3(pset):
                return psum[:, 3 * pset:3 * pset + 3, 0:CH]

            def cols3(ap):
                return ap.rearrange("p (c n) -> p c n", c=3)

            def times_r(job, pset, out):
                dve.wait_ge(tile_done, job + 1)
                dve.tensor_tensor(cols3(out), tile3(pset), r_3, ALU.mult).then_inc(tile_evacuated, 1)

            def late_squares(p, m):
                n = DVE_SUMS * p
                dve.wait_ge(square_ready, KD * p + m + 1)
                if m > 5:
                    dve.wait_ge(squares_summed, n + m - 5)
                dve.tensor_tensor(square[4], square[4], square[m], ALU.add).then_inc(squares_summed, 1)
                if m == KD - 1:
                    dve.wait_ge(squares_summed, n + 3)
                    dve.wait_ge(early_sum, POOL_SUMS * (p + 1))
                    dve.tensor_tensor(sumsq[:, 0:COLS], sumsq[:, 0:COLS], square[4],
                                      ALU.add).then_inc(squares_summed, 1)

            def xg_low(p, m):
                dve.wait_ge(xg_hi_ready, KD * p + m + 1)
                dve.scalar_tensor_tensor(lo_t[:, m, :], x_t[:, m, :], cst("gain", p * KD + m),
                                         hi_t[:, m, :].bitcast(F32), ALU.mult,
                                         ALU.subtract).then_inc(xg_ready, 1)

            def clear_pad():
                dve.memset(sumsq[:, COLS:ROW_TILES * P], 0.0).then_inc(pad_cleared, 1)

            def add_down(job, pset, m, loaded=None):
                if loaded is not None:
                    dve.wait_ge(x_loaded[m], loaded)
                dve.wait_ge(tile_done, job + 1)
                dve.wait_ge(tile_evacuated, evacuated(job - 1))
                dve.tensor_tensor(cols3(x_t[:, m, :]), tile3(pset), cols3(x_t[:, m, :]),
                                  ALU.add).then_inc(tile_evacuated, 1)

            def last_down(p, job, pset):
                clear_pad()
                for m in range(KD):
                    add_down(job + m, (pset + m) % 2, m)
                    if m >= 1:
                        if p + 1 < 4:
                            xg_low(p + 1, m - 1)
                        if m >= 6:
                            late_squares(p + 1, m - 1)
                if p + 1 < 4:
                    xg_low(p + 1, KD - 1)
                late_squares(p + 1, KD - 1)

            def rms(p, tail):
                dve.wait_ge(stats_ready, p + 1)
                dve.tensor_scalar(mean_sq[:], psum[:, tail, CH + 2:CH + 2 + ROW_TILES], 1.0 / D, EPS, ALU.mult,
                                  ALU.add).then_inc(mean_sq_ready, 1)
                dve.wait_ge(r_spread, p + 1)
                dve.tensor_copy(r_rows[:, 0:1024], psum[:, 6:8, :].rearrange("p a b -> p (a b)")).then_inc(r_ready, 1)
                dve.tensor_copy(r_rows[:, 1024:COLS],
                                psum[:, tail, CH + 30:CH + 30 + COLS - 1024]).then_inc(r_ready, 1)
                dve.wait_ge(r_ready, 2 * (p + 1))

            def conv3(t, par, w_at, w_name, state_at, state_name, new, new_at):
                g = conv_in[par]
                last_frames = g[:, 992:1060].rearrange("p (a b) -> p a b", b=34)[:, :, 32:34]
                dve.tensor_scalar(new[:, bass.ds(new_at, 4)].rearrange("p (a b) -> p a b", a=2), last_frames,
                                  1.0, None, ALU.mult).then_inc(state_saved, 1)
                dve.tensor_scalar(g[:, SAMPLE:SAMPLE + 2], cst(state_name, state_at, 2), 1.0, None,
                                  ALU.mult).then_inc(history_set, 1)
                dve.wait_ge(history_set, t + 1)
                dve.tensor_scalar(conv_out[par], g[:, 0:COLS], cst(w_name, w_at), None,
                                  ALU.mult).then_inc(conv_tap, 1)
                for k in (1, 2):
                    dve.wait_ge(conv_tap, t * 3 + k)
                    dve.scalar_tensor_tensor(conv_out[par], g[:, k:k + COLS], cst(w_name, w_at + k), conv_out[par],
                                             ALU.mult, ALU.add).then_inc(conv_tap, 1)

            def hidden_lo(a, par, slot):
                dve.wait_ge(act_hi_ready, a + 1)
                dve.tensor_tensor(al_t[:, slot, :], prod[par], ah_t[:, slot, :].bitcast(F32),
                                  ALU.subtract).then_inc(act_ready, 1)

            dve.wait_ge(const_loaded, 16)
            clear_pad()
            dve.memset(mv[:], 0.0).then_inc(pad_cleared, 1)
            dve.memset(var_eps[:], 1.0).then_inc(pad_cleared, 1)
            for m in range(KD):
                xg_low(0, m)
            for m in range(5, KD):
                late_squares(0, m)
            dve.wait_ge(squares_summed, DVE_SUMS)
            for c in range(4):
                dve.memset(a_in[c][:, 0:HA], 0.0).then_inc(glu_written, 1)
            dve.wait_ge(stats_ready, 1)
            dve.tensor_scalar(mean_sq_s[0:DEC, :], psum[0:DEC, 0, CH + 20:CH + 21], 1.0 / D, EPS, ALU.mult, ALU.add)
            rms(0, 0)

            def tap(c, k):
                acc_s = conv_s[:, c * DEC:(c + 1) * DEC]
                if k < DVE_TAPS:
                    w = cst("conv_a_w", c * TAPS_A + k)
                    src, src_s = a_in[c][:, k:k + SEQ], a_in[c][:, AO_SAMPLE + k:AO_SAMPLE + k + DEC]
                if k == 0:
                    dve.wait_ge(glu_written, 4 * (c + 2))
                    if c:
                        dve.wait_ge(a_conv_done, 2 * c)
                    b = cst("conv_a_b", c)
                    dve.tensor_scalar(conv_acc, src, w, b, ALU.mult, ALU.add).then_inc(a_tap, 1)
                    dve.tensor_scalar(acc_s, src_s, w, b, ALU.mult, ALU.add).then_inc(a_acc_s, 1)
                elif k < DVE_TAPS:
                    dve.wait_ge(a_tap, DVE_TAPS * c + k)
                    dve.scalar_tensor_tensor(conv_acc, src, w, conv_acc, ALU.mult, ALU.add).then_inc(a_tap, 1)
                    dve.wait_ge(a_acc_s, DVE_TAPS * c + k)
                    dve.scalar_tensor_tensor(acc_s, src_s, w, acc_s, ALU.mult, ALU.add).then_inc(a_acc_s, 1)
                else:
                    dve.wait_ge(a_tap, DVE_TAPS * (c + 1))
                    dve.wait_ge(a_acc_s, DVE_TAPS * (c + 1))
                    dve.wait_ge(a_pool_sum, (POOL_TAPS - 1) * (c + 1))
                    part = pool_sum[c % 2]
                    dve.tensor_tensor(a_out[c][:, 0:SEQ], conv_acc, part[:, 0:SEQ], ALU.add).then_inc(a_conv_done, 1)
                    dve.tensor_tensor(a_out[c][:, AO_SAMPLE:AO_SAMPLE + DEC], acc_s,
                                      part[:, AO_SAMPLE:AO_SAMPLE + DEC], ALU.add).then_inc(a_conv_done, 1)

            def taps(first, end):
                for step in range(first, end):
                    tap(step // (DVE_TAPS + 1), step % (DVE_TAPS + 1))

            def glu(c):
                a = a_in[c]
                dve.wait_ge(sigmoid_done, c + 1)
                dve.tensor_tensor(a[:, HA:HA + SEQ], tmp[0][:, 0:SEQ], tmp[1][:, 0:SEQ],
                                  ALU.mult).then_inc(glu_written, 1)
                dve.tensor_tensor(a[:, A_COLS - DEC:A_COLS], tmp[0][:, SAMPLE:SAMPLE + DEC],
                                  tmp[1][:, SAMPLE:SAMPLE + DEC], ALU.mult).then_inc(glu_written, 1)
                dve.tensor_copy(a[:, HA + SEQ:HA + SEQ + HA], cst("state_a", c * HA, HA)).then_inc(glu_written, 1)
                dve.wait_ge(glu_written, 4 + 4 * c + 3)
                last_frames = a[:, 992:A_COLS].rearrange("p (a b) -> p a b", b=62)[:, :, 32:62]
                dve.tensor_copy(new_a[:, c * 2 * HA:(c + 1) * 2 * HA].rearrange("p (a b) -> p a b", a=2),
                                last_frames).then_inc(glu_written, 1)

            mv_t = mv[:].rearrange("p (t s) -> p t s", s=2)

            def row_moment(seen, t, rows):
                n = P if t < 8 else DEC
                dve.bn_stats(bn[0:n, 6 * t:6 * t + 6], rows).then_inc(row_stats, 1)
                dve.wait_ge(row_stats, seen + 1)
                dve.bn_aggr(mv[0:n, 2 * t:2 * t + 2], bn[0:n, 6 * t:6 * t + 6]).then_inc(row_moments, 1)

            def neg_mean_rstd(n):
                dve.wait_ge(rstd_ready, n)
                dve.scalar_tensor_tensor(neg_mean[:], mv_t[:, :, 0], -1.0, rstd[:], ALU.mult,
                                         ALU.mult).then_inc(neg_mean_ready, 1)

            def v_statistics():
                dve.wait_ge(v_evacuated, 8)
                dve.wait_ge(pad_cleared, 3)
                for t in range(ROW_TILES):
                    row_moment(t, t, v_rows[0:P if t < 8 else DEC, t, :])
                dve.wait_ge(row_moments, ROW_TILES)
                dve.scalar_tensor_tensor(var_eps[:, 0:8], mean_sq[:, 0:8], EPS, mv_t[:, 0:8, 1], ALU.mult, ALU.add)
                dve.scalar_tensor_tensor(var_eps[0:DEC, 8:9], mean_sq_s[0:DEC, :], EPS, mv_t[0:DEC, 8:9, 1],
                                         ALU.mult, ALU.add).then_inc(var_ready, 1)

            def v_sample():
                dve.wait_ge(v_ready, ROW_TILES)
                dve.wait_ge(mix_loaded, 48)
                dve.tensor_tensor(lnv_g, lnv_g, v_rows[0:DEC, 8, :], ALU.mult).then_inc(v_sample_ready, 1)
                dve.wait_ge(v_sample_ready, 1)
                dve.tensor_tensor(lnv_g, lnv_g, lnv_b, ALU.add).then_inc(v_sample_ready, 1)

            def mixed(c):
                s = 3 * (JOB_S[c] % 2)
                g, b = cst("ln_v_g", c), cst("ln_v_b", c)
                dve.wait_ge(tile_done, JOB_S[c] + 1)
                dve.scalar_tensor_tensor(mix_bias[:, 0:P], psum[:, s + 2, DEC:DEC + P], b, mix_b[:, c, :],
                                         ALU.mult, ALU.add).then_inc(mix_bias_ready, 1)
                dve.scalar_tensor_tensor(mix_bias[:, P:P + DEC], psum[:, s + 2, DEC + P:2 * DEC + P], b,
                                         mix_b[:, c, 0:DEC], ALU.mult, ALU.add).then_inc(mix_bias_ready, 1)
                dve.wait_ge(mix_bias_ready, 2 * (c + 1))
                dve.scalar_tensor_tensor(tmp[1][:, 0:SEQ].rearrange("p (n i) -> p n i", i=P),
                                         psum[:, s:s + 2, :].rearrange("p a (b i) -> p (a b) i", i=P), g,
                                         mix_bias[:, 0:P].rearrange("p (a i) -> p a i", a=1).to_broadcast([P, 8, P]),
                                         ALU.mult, ALU.add)
                dve.scalar_tensor_tensor(tmp[1][:, SAMPLE:SAMPLE + DEC], psum[:, s + 2, 0:DEC], g,
                                         mix_bias[:, P:P + DEC], ALU.mult, ALU.add).then_inc(tile_evacuated, 1)
                dve.wait_ge(tile_evacuated, evacuated(JOB_S[c]))
                dve.tensor_tensor(tmp[1], tmp[1], r_rows[:], ALU.mult).then_inc(mix_times_r, 1)

            def gated_b(c):
                job = JOB_S[c] + 1
                dve.wait_ge(tile_done, job + 1)
                dve.wait_ge(mix_times_r, c + 1)
                dve.tensor_tensor(cols3(tmp[0]), tile3(job % 2), cols3(tmp[1]),
                                  ALU.mult).then_inc(tile_evacuated, 1)

            def b_low(c):
                dve.wait_ge(act_hi_ready, c + 1)
                dve.tensor_tensor(al_t[:, c, :], tmp[0], ah_t[:, c, :].bitcast(F32),
                                  ALU.subtract).then_inc(act_ready, 1)

            times_r(0, 0, tmp[0])
            times_r(1, 1, tmp[1])
            glu(0)
            taps(0, 3)
            times_r(2, 0, tmp[0])
            taps(3, 9)
            times_r(3, 1, tmp[1])
            taps(9, 11)
            glu(1)
            taps(11, 14)
            times_r(4, 0, tmp[0])
            taps(14, 20)
            times_r(5, 1, tmp[1])
            taps(20, 22)
            glu(2)
            dve.wait_ge(mix_loaded, 48)
            dve.memset(mix_w[64:P, :, 0:64], 0.0).then_inc(mask_set, 1)
            taps(22, 51)
            v_statistics()
            taps(51, 53)
            neg_mean_rstd(1)
            times_r(14, 0, tmp[0])
            taps(53, 58)
            v_sample()
            times_r(15, 1, tmp[1])
            taps(58, 60)
            glu(3)
            step = 60
            for c in range(4):
                mixed(c)
                taps(step, step + 5)
                gated_b(c)
                if c < 3:
                    taps(step + 5, step + 6)
                b_low(c)
                step += 6
            taps(step - 1, 4 * (DVE_TAPS + 1))
            for m in range(ROWS_FROM):
                add_down(JOB_DOWN_B + m, m % 2, m, loaded=32)
            for t in range(ROW_TILES):
                dve.wait_ge(a_rows_ready, t + 1)
                row_moment(ROW_TILES + t, t, psum[0:P if t < 8 else DEC, 6 + t % 2, :])
                if t in (3, 7):
                    m = ROWS_FROM + t // 4
                    add_down(JOB_DOWN_B + m, m % 2, m, loaded=32)
            dve.wait_ge(row_moments, 2 * ROW_TILES)
            dve.tensor_scalar(var_eps[:], mv_t[:, :, 1], EPS, None, ALU.add).then_inc(var_ready, 1)
            neg_mean_rstd(2)

            def a_scale(c):
                dve.wait_ge(ln_copied, 1)
                dve.tensor_tensor(a_out[c], a_out[c], tap_prod[0], ALU.mult).then_inc(a_scaled, 1)

            def a_shift(c):
                dve.wait_ge(a_scaled, c + 1)
                dve.wait_ge(ln_copied, 2)
                dve.tensor_tensor(a_out[c], a_out[c], tap_prod[1], ALU.add).then_inc(a_normed, 1)

            def a_low(c):
                dve.wait_ge(act_hi_ready, 4 + c + 1)
                dve.tensor_tensor(al_t[:, c, 0:SEQ], a_out[c][:, 0:SEQ], ah_t[:, c, 0:SEQ].bitcast(F32),
                                  ALU.subtract)
                dve.tensor_tensor(al_t[:, c, SAMPLE:SAMPLE + DEC], a_out[c][:, AO_SAMPLE:AO_SAMPLE + DEC],
                                  ah_t[:, c, SAMPLE:SAMPLE + DEC].bitcast(F32), ALU.subtract).then_inc(act_ready, 1)

            add_down(JOB_DOWN_B + 4, 0, 4, loaded=32)
            add_down(JOB_DOWN_B + 5, 1, 5, loaded=32)
            for c in range(4):
                a_scale(c)
            a_shift(0)
            add_down(JOB_DOWN_B + 6, 0, 6, loaded=32)
            for c in range(1, 4):
                a_shift(c)
            for c in range(4):
                a_low(c)
            add_down(JOB_DOWN_B + 7, 1, 7, loaded=32)
            last_down(0, JOB_DOWN_A, 0)

            def clear_history():
                for g in conv_in:
                    dve.memset(g[:, 0:2], 0.0)

            def gate_tile(l, job, pset, t, f, par):
                times_r(job, pset, conv_in[par][:, 2:])
                dve.wait_ge(tile_evacuated, evacuated(job))
                at_f = f + l * FF_TILES
                conv3(t, par, at_f * 3, "conv_f_w", at_f * 2, "state_f", new_f, at_f * 4)

            def up_tile(job, pset, s, par):
                times_r(job, pset, prod[par])
                dve.wait_ge(tile_evacuated, evacuated(job))
                dve.wait_ge(silu_done, s + 1)
                dve.tensor_tensor(prod[par], prod[par], factor[par], ALU.mult).then_inc(product_done, 1)

            def ffn(p):
                l = (p - 1) // 2
                job, a0, t0 = JOB0[p], ACT0[p], CONV0[p]
                f0 = l * FF_TILES
                s0 = job % 2
                rms(p, 3 * s0)
                clear_history()
                gate_tile(l, job, s0, t0, 0, 0)
                up_tile(job + 1, 1 - s0, f0, 0)
                hidden_lo(a0, 0, 0)
                gate_tile(l, job + 2, s0, t0 + 1, 1, 1)
                up_tile(job + 3, 1 - s0, f0 + 1, 1)
                hidden_lo(a0 + 1, 1, 1)
                with dve.Fori(0, (FF_BLOCKS - 1) // 2) as i:
                    for b in range(2):
                        j = i * 24 + (job + 4 + 12 * b)
                        for q in range(2):
                            f = 2 + 2 * b + q
                            gate_tile(l, j + 2 * q, s0, i * 4 + (t0 + f), i * 4 + f, q)
                            up_tile(j + 2 * q + 1, 1 - s0, i * 4 + (f0 + f), q)
                            if q == 0:
                                hidden_lo(i * 4 + (a0 + f), q, f % 4)
                        add_down(j + 4, s0, 0)
                        hidden_lo(i * 4 + (a0 + 3 + 2 * b), 1, (3 + 2 * b) % 4)
                        for m in range(1, KD):
                            add_down(j + 4 + m, (s0 + m) % 2, m)
                last_down(p, job + FF_JOBS - 8, s0)

            ffn(1)
            p = 2
            s0 = JOB0[p] % 2
            rms(p, 3 * s0)
            clear_history()

            def c_tile(job, c):
                par = c % 2
                sets = [(job + q) % 2 for q in range(3)]
                times_r(job, sets[0], factor[par])
                times_r(job + 1, sets[1], prod[par])
                dve.wait_ge(tile_evacuated, evacuated(job + 1))
                dve.tensor_tensor(conv_in[par][:, 2:], factor[par], prod[par], ALU.mult).then_inc(factor_ready, 1)
                dve.wait_ge(factor_ready, c + 1)
                conv3(CONV0[p] + c, par, c * 3, "conv_c_w", c * 2, "state_c", new_c, c * 4)
                times_r(job + 2, sets[2], prod[par])
                dve.wait_ge(tile_evacuated, evacuated(job + 2))
                dve.wait_ge(conv_tap, 3 * (CONV0[p] + c + 1))
                dve.tensor_tensor(prod[par], prod[par], conv_out[par], ALU.mult).then_inc(product_done, 1)

            for half in range(2):
                job = JOB0[p] + 28 * half
                for t in range(4):
                    c = 4 * half + t
                    c_tile(job + 3 * t, c)
                    if t < 3:
                        hidden_lo(ACT0[p] + c, c % 2, t)
                for m in range(KD):
                    add_down(job + 12 + m, (s0 + m) % 2, m)
                    if m == 0:
                        hidden_lo(ACT0[p] + 4 * half + 3, 1, 3)
                if half == 0:
                    for m in range(KD):
                        add_down(job + 20 + m, (s0 + m) % 2, m)
                else:
                    last_down(p, job + 20, s0)
            ffn(3)
            rms(4, 0)
            for m in (m for m in range(KD) if m not in POOL_Y):
                dve.scalar_tensor_tensor(x_t[:, m, :], x_t[:, m, :], cst("gain", 4 * KD + m), r_rows[:],
                                         ALU.mult, ALU.mult).then_inc(y_ready, 1)


POOL_Y = [3, 6]


A_PLAN = {2: [(0, 0, 3)], 3: [(0, 3, 6)], 4: [(0, 6, 9)], 5: [(0, 9, 10), (1, 0, 3)], 6: [(1, 3, 6)],
          7: [(1, 6, 9)], 8: [(1, 9, 10), (2, 0, 3)], 9: [(2, 3, 6)], 10: [(2, 6, 8)], 11: [(2, 8, 10)],
          12: [(3, 0, 3)], 13: [(3, 3, 6)], 14: [(3, 6, 9)], 15: [(3, 9, 10)]}


def _pack(inputs):
    def cols(a):
        a = np.asarray(a)
        lead = a.reshape(-1, a.shape[-1] // P, P)
        return lead.transpose(2, 1, 0).reshape(P, -1)

    i = {k: np.asarray(v) for k, v in inputs.items()}
    xt = np.zeros((D, COLS), np.float32)
    xt[:, 0:SEQ] = i["x_prompt"][0].T
    xt[:, SAMPLE:SAMPLE + DEC] = i["x_sample"][0].T

    def up(w, t):
        return w[:, t * P:(t + 1) * P].reshape(KD, P, P).transpose(1, 0, 2).reshape(P, SLAB)

    def down(w, row, n_k, s):
        n_m = 8 // n_k
        part = w[row:row + n_k * P, s * n_m * P:(s + 1) * n_m * P]
        return part.reshape(n_k, P, n_m, P).transpose(1, 2, 0, 3).reshape(P, SLAB)

    slabs = []
    w, wo = i["w_in_ab"][0], i["w_out_ab"][0]
    order = [0, 4, 1, 5, 2, 6] + [12, 13, 14, 15] + [3, 7] + [8, 9, 10, 11]
    slabs += [up(w, t) for t in order]
    slabs += [down(wo, AW, 4, s) for s in range(4)] + [down(wo, 0, 4, s) for s in range(4)]

    def ffn(l):
        w, wd = i["w_up"][l], i["w_down"][l]
        for b in range(FF_BLOCKS):
            for f in (2 * b, 2 * b + 1):
                slabs.extend([up(w, f), up(w, FF_TILES + f)])
            if b:
                slabs.extend(down(wd, 2 * (b - 1) * P, 2, s) for s in range(2))
        slabs.extend(down(wd, 2 * (FF_BLOCKS - 1) * P, 2, s) for s in range(2))

    ffn(0)
    w, wo = i["w_in_c"][0], i["w_out_c"][0]
    for half in range(2):
        for c in range(4 * half, 4 * half + 4):
            slabs += [up(w, KD + c), up(w, 2 * KD + c), up(w, c)]
        for b in (2 * half, 2 * half + 1):
            slabs += [down(wo, 2 * b * P, 2, s) for s in range(2)]
    ffn(1)
    slabs = np.stack(slabs)
    assert slabs.shape[0] == N_SLABS

    gains = [i["norm_mix"][0], i["norm_ffn"][0], i["norm_mix"][1], i["norm_ffn"][1], i["norm_final"]]
    parts = {
        "gain": np.concatenate([cols(g) for g in gains], 1),
        "conv_a_w": cols(i["conv_a_w"][0]), "conv_a_b": cols(i["conv_a_b"][0]),
        "ln_v_g": cols(i["ln_v_g"][0]), "ln_v_b": cols(i["ln_v_b"][0]),
        "ln_a_g": cols(i["ln_a_g"][0]), "ln_a_b": cols(i["ln_a_b"][0]), "state_a": cols(i["state_conv_a"][0, 0]),
        "conv_c_w": cols(i["conv_c_w"][0]), "state_c": cols(i["state_conv_c"][0, 0]),
        "conv_f_w": np.concatenate([cols(i["conv_f_w"][l]) for l in range(2)], 1),
        "state_f": np.concatenate([cols(i["state_ffn"][l, 0]) for l in range(2)], 1),
    }
    consts = np.concatenate([parts[n] for n, _ in _SIZES], 1)
    assert consts.shape == (P, N_CONST)
    mix = i["ws_b"][0].transpose(2, 0, 1).reshape(P, 8 * P)
    bs = np.repeat(i["bs_b"][0].reshape(4, 2, P), 64, axis=1)
    bs = bs.transpose(1, 0, 2).reshape(P, 4 * P)
    lnv = np.tile(np.concatenate([i["ln_v_g"][0], i["ln_v_b"][0]])[None], (DEC, 1))
    return [("x_t", xt), ("slabs", slabs), ("consts", consts), ("mix", mix), ("bs", bs), ("lnv", lnv)]


_OUTS = [("y_t", (D, COLS)), ("a_state", (P, 4 * 2 * HA)), ("c_state", (P, KD * 4)),
         ("f_state", (P, 2 * FF_TILES * 4)), ("v_rows_out", (DEC, AW))]


def kernel(**inputs):
    import concourse.bacc as bacc
    from concourse.bass_utils import run_bass_kernel_spmd

    nc = bacc.Bacc("TRN2", target_bir_lowering=False, num_devices=1)
    arrays, args = {}, []
    for name, a in _pack(inputs):
        a = np.ascontiguousarray(a)
        arrays[name] = a
        args.append(nc.dram_tensor(name, a.shape, mybir.dt.from_np(a.dtype), kind="ExternalInput").ap())
    for name, shape in _OUTS:
        args.append(nc.dram_tensor(name, shape, F32, kind="ExternalOutput").ap())
    build(nc, *args)
    got = run_bass_kernel_spmd(nc, [arrays], core_ids=[0]).results[0]

    def rows(a, tiles, n):
        a = np.asarray(a).reshape(P, tiles, 2, n).transpose(2, 3, 1, 0).reshape(2, n, tiles * P)
        return a[0], a[1]

    y = np.asarray(got["y_t"])
    y_prompt = np.ascontiguousarray(y[:, 0:SEQ].T)[None]
    y_sample = np.ascontiguousarray(y[:, SAMPLE:SAMPLE + DEC].T)[None]
    a_p, a_s = rows(got["a_state"], 4, HA)
    c_p, c_s = rows(got["c_state"], KD, 2)
    f = np.asarray(got["f_state"]).reshape(P, 2, FF_TILES * 4)
    f_ps = [rows(np.ascontiguousarray(f[:, l]), FF_TILES, 2) for l in range(2)]
    f_p = np.stack([q[0][None] for q in f_ps])
    f_s = np.stack([q[1][None] for q in f_ps])
    v = np.asarray(got["v_rows_out"])[None, None]
    return (y_prompt, y_sample, a_p[None, None], a_s[None, None], c_p[None, None], c_s[None, None], f_p, f_s, v)
```

```python
import numpy as np

import concourse.bass as bass
from concourse import mybir
from contextlib import ExitStack

F32 = mybir.dt.float32
F32R = mybir.dt.float32r
ALU = mybir.AluOpType
ACT = mybir.ActivationFunctionType

P = 128
D = 1024
SEQ = 1024
DEC = 32
DFF = 2816
AW = 512
TAPS_A = 31
EPS = 1e-6

KD = D // P
SAMPLE = SEQ + 2
COLS = 1062
CH = COLS // 3
ROW_TILES = 9
FF_TILES = DFF // P
FF_BLOCKS = FF_TILES // 2
SLAB = 8 * P

HA = TAPS_A - 1
A_COLS = HA + SEQ + HA + DEC
AO_COLS = A_COLS - HA
AO_SAMPLE = SEQ + HA
POOL_TAPS = 10
DVE_TAPS = TAPS_A - POOL_TAPS

_SIZES = [("gain", 5 * KD), ("conv_a_w", 4 * TAPS_A), ("conv_a_b", 4), ("ln_a_g", 4), ("ln_a_b", 4),
          ("ln_v_g", 4), ("ln_v_b", 4), ("state_a", 4 * HA), ("conv_c_w", KD * 3), ("state_c", KD * 2),
          ("conv_f_w", 2 * FF_TILES * 3), ("state_f", 2 * FF_TILES * 2)]
OFF = {}
_at = 0
for _name, _size in _SIZES:
    OFF[_name] = _at
    _at += _size
N_CONST = _at

AB_SLABS = 24
JOB_A = [0, 2, 4, 14]
JOB_V = [6, 7, 9, 11]
JOB_VT = [8, 10, 12, 13]
JOB_S = [16, 18, 20, 22]
JOB_DOWN_B = 24
JOB_DOWN_A = 32
AB_JOBS = 40
ROWS_STEP = 9
SPREAD_STEP = 21
CH_ROWS = CH // 3
DVE_Y = 5
FF_SLABS = 6 * FF_BLOCKS
FF_JOBS = 12 * FF_BLOCKS
C_SLABS = 32
C_JOBS = 56

JOB0 = [0, AB_JOBS, AB_JOBS + FF_JOBS, AB_JOBS + FF_JOBS + C_JOBS]
SLAB0 = [0, AB_SLABS, AB_SLABS + FF_SLABS, AB_SLABS + FF_SLABS + C_SLABS]
N_SLABS = AB_SLABS + 2 * FF_SLABS + C_SLABS
N_JOBS = JOB0[3] + FF_JOBS
FINAL_JOB = N_JOBS - KD
assert FINAL_JOB % 2 == 0


def _jobs_after_slab():
    after = []
    for c in (0, 1, 2):
        after += [JOB_A[c] + 1, JOB_A[c] + 2]
    after += [j + 1 for j in JOB_V]
    after += [JOB_A[3] + 1, JOB_A[3] + 2]
    after += [j + 2 for j in JOB_S]
    after += [JOB_DOWN_B + 2 * (s + 1) for s in range(4)]
    after += [JOB_DOWN_A + 2 * (s + 1) for s in range(4)]
    for phase in (1, 2, 3):
        at = JOB0[phase]
        if phase == 2:
            steps = ([1] * 12 + [4] * 4) * 2
        else:
            steps = [1] * 4 + ([1] * 4 + [4, 4]) * (FF_BLOCKS - 1) + [4, 4]
        for s in steps:
            at += s
            after.append(at)
    return after


AFTER = _jobs_after_slab()


def evacuated(job):
    return job + 1 if isinstance(job, int) and job < JOB_V[0] else job - 7


POOL_SUMS = 3
DVE_SUMS = KD - POOL_SUMS - 1


ACT0 = [0, 8, 8 + FF_TILES, 8 + FF_TILES + KD]
CONV0 = [None, 0, FF_TILES, FF_TILES + KD]


def build(nc, x_in, slabs, consts_in, mix_in, bs_in, lnv_in, y_out, a_state, c_state, f_state, v_out):
    with ExitStack() as ctx:
        def sb(name, cols, dt=F32):
            return ctx.enter_context(nc.sbuf_tensor(name, [P, cols], dt))

        def sem(name):
            return ctx.enter_context(nc.semaphore(name))

        x = sb("x", KD * COLS)
        xg_hi = sb("xg_hi", KD * COLS, F32R)
        xg_lo = sb("xg_lo", KD * COLS, F32R)
        act_hi = sb("act_hi", 4 * COLS, F32R)
        act_lo = sb("act_lo", 4 * COLS, F32R)
        raw = sb("raw", 2 * SLAB)
        w_hi = sb("w_hi", 2 * SLAB, F32R)
        w_lo = sb("w_lo", 2 * SLAB, F32R)
        r_rows = sb("r_rows", COLS)
        sumsq = sb("sumsq", ROW_TILES * P)
        work = sb("work", 4 * A_COLS + 2 * COLS + 2 * AO_COLS)
        const = sb("const", N_CONST)
        ident = sb("ident", P)
        ones = sb("ones", 64)
        minus_half = sb("minus_half", ROW_TILES)
        mean_sq = sb("mean_sq", ROW_TILES)
        mean_sq_s = sb("mean_sq_s", 1)
        r_col = sb("r_col", ROW_TILES)
        bn = sb("bn", ROW_TILES * 6)
        mv = sb("mv", ROW_TILES * 2)
        var_eps = sb("var_eps", ROW_TILES)
        rstd = sb("rstd", ROW_TILES)
        neg_mean = sb("neg_mean", ROW_TILES)
        conv_s = sb("conv_s", 4 * DEC)
        mix_bias = sb("mix_bias", P + DEC)
        new_a = sb("new_a", 4 * 2 * HA)
        new_c = sb("new_c", KD * 4)
        new_f = sb("new_f", 2 * FF_TILES * 4)
        psum = ctx.enter_context(nc.psum_tensor("psum", [P, 8, 512], F32))

        def cst(name, at, n=1):
            return const[:, bass.ds(OFF[name] + at, n)]

        x_t = x[:].rearrange("p (m n) -> p m n", m=KD)
        hi_t = xg_hi[:].rearrange("p (m n) -> p m n", m=KD)
        lo_t = xg_lo[:].rearrange("p (m n) -> p m n", m=KD)
        ah_t = act_hi[:].rearrange("p (m n) -> p m n", m=4)
        al_t = act_lo[:].rearrange("p (m n) -> p m n", m=4)
        r_3 = r_rows[:].rearrange("p (c n) -> p c n", c=3)

        GW = COLS + 2
        conv_in = [work[:, i * GW:(i + 1) * GW] for i in range(2)]
        conv_out = [work[:, (2 + i) * GW:(2 + i) * GW + COLS] for i in range(2)]
        factor = [work[:, (4 + i) * GW:(4 + i) * GW + COLS] for i in range(2)]
        prod = [work[:, (6 + i) * GW:(6 + i) * GW + COLS] for i in range(2)]
        a_in = [work[:, c * A_COLS:(c + 1) * A_COLS] for c in range(4)]
        a_out = [work[:, c * A_COLS:c * A_COLS + AO_COLS] for c in range(4)]
        tmp = [work[:, 4 * A_COLS + i * COLS:4 * A_COLS + (i + 1) * COLS] for i in range(2)]
        at = 4 * A_COLS + 2 * COLS
        tap_prod = [sumsq[:, 0:AO_COLS], work[:, at:at + AO_COLS]]
        conv_acc = psum[:, 6:8, :].rearrange("p a b -> p (a b)")
        square = [work[:, m * COLS:(m + 1) * COLS] for m in range(KD)]
        v_rows = x[:, 0:ROW_TILES * AW].rearrange("p (t f) -> p t f", t=ROW_TILES)
        at = ROW_TILES * AW
        mix_w = x[:, at:at + 8 * P].rearrange("p (g i) -> p g i", g=8)
        at += 8 * P
        mix_b = x[:, at:at + 4 * P].rearrange("p (c i) -> p c i", c=4)
        at += 4 * P
        lnv_g = x[0:DEC, at:at + AW]
        lnv_b = x[0:DEC, at + AW:at + 2 * AW]
        lnv = x[0:DEC, at:at + 2 * AW]
        assert at + 2 * AW <= KD * COLS - AO_COLS
        pool_sum = [x[:, KD * COLS - AO_COLS:KD * COLS], work[:, 4 * A_COLS + 2 * COLS + AO_COLS:]]

        gains_loaded = sem("gains_loaded")
        const_loaded = sem("const_loaded")
        x_loaded = [sem(f"x_loaded{m}") for m in range(KD)]
        mix_loaded = sem("mix_loaded")
        raw_loaded = [sem(f"raw_loaded{i}") for i in range(2)]
        weights_hi = sem("weights_hi")
        weights_ready = sem("weights_ready")
        consts_made = sem("consts_made")
        pad_cleared = sem("pad_cleared")
        tile_done = sem("tile_done")
        tile_evacuated = sem("tile_evacuated")
        xg_hi_ready = sem("xg_hi_ready")
        xg_ready = sem("xg_ready")
        square_ready = sem("square_ready")
        squares_summed = sem("squares_summed")
        stats_ready = sem("stats_ready")
        mean_sq_ready = sem("mean_sq_ready")
        r_col_ready = sem("r_col_ready")
        r_spread = sem("r_spread")
        r_ready = sem("r_ready")
        state_saved = sem("state_saved")
        history_set = sem("history_set")
        conv_tap = sem("conv_tap")
        factor_ready = sem("factor_ready")
        product_done = sem("product_done")
        act_hi_ready = sem("act_hi_ready")
        act_ready = sem("act_ready")
        act_free = sem("act_free")
        sigmoid_done = sem("sigmoid_done")
        glu_written = sem("glu_written")
        a_tap = sem("a_tap")
        a_tap_product = sem("a_tap_product")
        a_pool_sum = sem("a_pool_sum")
        a_conv_done = sem("a_conv_done")
        a_acc_s = sem("a_acc_s")
        early_sum = sem("early_sum")
        v_evacuated = sem("v_evacuated")
        mix_bias_ready = sem("mix_bias_ready")
        mix_times_r = sem("mix_times_r")
        ln_spread = sem("ln_spread")
        ln_copied = sem("ln_copied")
        x_scaled = sem("x_scaled")
        y_ready_pool = sem("y_ready_pool")
        a_rows_ready = sem("a_rows_ready")
        row_stats = sem("row_stats")
        row_moments = sem("row_moments")
        var_eps_set = sem("var_eps_set")
        var_ready = sem("var_ready")
        rstd_ready = sem("rstd_ready")
        neg_mean_ready = sem("neg_mean_ready")
        v_ready = sem("v_ready")
        v_sample_ready = sem("v_sample_ready")
        mask_set = sem("mask_set")
        a_scaled = sem("a_scaled")
        a_scaled_pool = sem("a_scaled_pool")
        a_normed = sem("a_normed")
        a_silu_done = sem("a_silu_done")
        silu_done = sem("silu_done")
        y_ready = sem("y_ready")
        v_stored = sem("v_stored")
        stored = sem("stored")

        block = ctx.enter_context(nc.Block())

        @block.sync
        def _(sp):
            def load_slab(n, slot):
                sp.dma_start(raw[:, slot * SLAB:(slot + 1) * SLAB],
                             slabs[bass.ds(n, 1), :, :].rearrange("s p n -> p (s n)")).then_inc(raw_loaded[slot], 16)

            def load_slabs(first, end):
                for n in range(first, end):
                    sp.wait_ge(weights_ready, n - 1)
                    load_slab(n, n % 2)

            def load_x(m):
                sp.dma_start(x_t[:, m, :], x_in[m * P:(m + 1) * P, :]).then_inc(x_loaded[m], 16)

            load_slab(0, 0)
            gains = slice(OFF["gain"], OFF["gain"] + 5 * KD)
            sp.dma_start(const[:, gains], consts_in[:, gains]).then_inc(gains_loaded, 16)
            for m in range(KD):
                load_x(m)
                if m == 2:
                    load_slab(1, 1)
            others = slice(5 * KD, N_CONST)
            sp.dma_start(const[:, others], consts_in[:, others]).then_inc(const_loaded, 16)
            load_slabs(2, 4)
            sp.wait_ge(xg_ready, KD)
            sp.wait_ge(squares_summed, DVE_SUMS)
            sp.dma_start(mix_w, mix_in.rearrange("p (g i) -> p g i", g=8)).then_inc(mix_loaded, 16)
            sp.dma_start(mix_b, bs_in.rearrange("p (c i) -> p c i", c=4)).then_inc(mix_loaded, 16)
            sp.dma_start(lnv, lnv_in).then_inc(mix_loaded, 16)
            load_slabs(4, 14)
            sp.wait_ge(v_sample_ready, 2)
            sp.dma_start(v_out, lnv_g).then_inc(v_stored, 16)
            load_slabs(14, 18)
            sp.wait_ge(tile_evacuated, evacuated(JOB_S[3]))
            sp.wait_ge(v_stored, 16)
            sp.wait_ge(a_conv_done, 6)
            load_x(0)
            load_x(1)
            load_slabs(18, 19)
            load_x(2)
            load_x(3)
            load_slabs(19, 20)
            load_x(4)
            load_x(5)
            load_slabs(20, 21)
            load_x(6)
            load_x(7)
            load_slabs(21, 22)
            sp.wait_ge(glu_written, 20)
            sp.dma_start(a_state, new_a[:]).then_inc(stored, 16)
            with sp.Fori(11, N_SLABS // 2) as i:
                sp.wait_ge(weights_ready, i * 2 - 1)
                load_slab(i * 2, 0)
                sp.wait_ge(weights_ready, i * 2)
                load_slab(i * 2 + 1, 1)
            sp.wait_ge(state_saved, 2 * FF_TILES + KD)
            sp.dma_start(c_state, new_c[:]).then_inc(stored, 16)
            sp.dma_start(f_state, new_f[:]).then_inc(stored, 16)
            for c in range(3):
                for first, end in ((0, 2), (2, DVE_Y), (DVE_Y, KD)):
                    if end <= DVE_Y:
                        sp.wait_ge(y_ready, DVE_Y * c + end)
                    else:
                        sp.wait_ge(y_ready_pool, (KD - DVE_Y) * (c + 1))
                    cols = slice(c * CH, (c + 1) * CH)
                    sp.dma_start(y_out[first * P:end * P, cols].rearrange("(m p) n -> p m n", p=P),
                                 x_t[:, first:end, cols]).then_inc(stored, 16)
            sp.wait_ge(stored, 16 * (3 + 9))

        @block.tensor
        def _(pe):
            def split_product(out, w_at, slot, hi, lo, start, stop):
                s = slice(slot * SLAB + w_at * P, slot * SLAB + (w_at + 1) * P)
                nc.tensor.matmul(out, w_hi[:, s], hi, start=start, stop=False)
                nc.tensor.matmul(out, w_hi[:, s], lo, start=False, stop=False)
                return nc.tensor.matmul(out, w_lo[:, s], hi, start=False, stop=stop)

            def bank(pset, c):
                return psum[:, 3 * pset + c, 0:CH]

            def up_part(pset, slot, ks):
                last = None
                for k in ks:
                    for c in range(3):
                        cols = slice(c * CH, (c + 1) * CH)
                        last = split_product(bank(pset, c), k, slot, hi_t[:, k, cols], lo_t[:, k, cols],
                                             k == 0, k == KD - 1)
                return last

            def banks_free(job):
                if isinstance(job, int) and JOB_V[0] <= job - 2 <= JOB_VT[3]:
                    pe.wait_ge(v_evacuated, job - 2 - JOB_V[0] + 1)
                elif not isinstance(job, int) or job >= 2:
                    pe.wait_ge(tile_evacuated, evacuated(job - 2))

            def up_job(job, slab, pset, slot, fresh=None):
                banks_free(job)
                pe.wait_ge(weights_ready, slab + 1)
                if fresh is None:
                    up_part(pset, slot, range(KD)).then_inc(tile_done, 1)
                else:
                    for k in range(KD):
                        pe.wait_ge(xg_ready, KD * fresh + k + 1)
                        last = up_part(pset, slot, [k])
                    last.then_inc(tile_done, 1)

            def down_jobs(job, slab, acts, act0, n_k, pset, slot, between=None, free=False):
                pe.wait_ge(weights_ready, slab + 1)
                for m in range(8 // n_k):
                    banks_free(job + m)
                    for k in range(n_k):
                        if between is not None:
                            between(m, k)
                        if acts is not None and m == 0:
                            pe.wait_ge(act_ready, acts + k + 1)
                        for c in range(3):
                            cols = slice(c * CH, (c + 1) * CH)
                            last = split_product(bank((pset + m) % 2, c), m * n_k + k, slot,
                                                 ah_t[:, act0 + k, cols], al_t[:, act0 + k, cols],
                                                 k == 0, k == n_k - 1)
                        if free and m == 8 // n_k - 1 and k < n_k - 1:
                            last.then_inc(act_free, 1)
                    last.then_inc(tile_done, 1)

            def rms_stats(p, tail):
                pe.wait_ge(squares_summed, DVE_SUMS * (p + 1))
                if p == 0:
                    nc.tensor.matmul(psum[0:DEC, tail, CH + 20:CH + 21], sumsq[:, SAMPLE:SAMPLE + DEC],
                                     ones[:, 0:1], start=True, stop=True)
                for t in range(ROW_TILES):
                    last = nc.tensor.matmul(psum[:, tail, CH + 2 + t:CH + 3 + t], sumsq[:, t * P:(t + 1) * P],
                                            ones[:, 0:1], start=True, stop=True)
                last.then_inc(stats_ready, 1)

            def rms_spread(p, tail):
                pe.wait_ge(r_col_ready, p + 1)
                for t in range(ROW_TILES):
                    n = min(P, COLS - t * P)
                    out = psum[:, 6 + t // 4, (t % 4) * P:(t % 4 + 1) * P] if t < 8 else \
                        psum[:, tail, CH + 30:CH + 30 + n]
                    last = nc.tensor.matmul(out, r_col[:, t:t + 1].to_broadcast([P, P]), ident[:, 0:n],
                                            start=True, stop=True)
                last.then_inc(r_spread, 1)

            def phase_start(p):
                job, slab = JOB0[p], SLAB0[p]
                a, b = job % 2, (job + 1) % 2
                early, late = (4, 6) if p == 0 else (0, 5)
                up_job(job, slab, a, slab % 2, fresh=p)
                banks_free(job + 1)
                pe.wait_ge(weights_ready, slab + 2)
                up_part(b, (slab + 1) % 2, range(0, early))
                rms_stats(p, 3 * a)
                up_part(b, (slab + 1) % 2, range(early, late))
                rms_spread(p, 3 * a)
                up_part(b, (slab + 1) % 2, range(late, KD)).then_inc(tile_done, 1)

            def turn_v(c):
                job = JOB_VT[c]
                s = 3 * (job % 2)
                pe.wait_ge(v_evacuated, JOB_V[c] - JOB_V[0] + 1)
                banks_free(job)
                for t in range(8):
                    nc.tensor.transpose(psum[:, s + t // 4, (t % 4) * P:(t % 4 + 1) * P],
                                        tmp[c % 2][:, t * P:(t + 1) * P], ident[:])
                nc.tensor.transpose(psum[0:DEC, s + 2, 0:P], tmp[c % 2][:, SAMPLE:SAMPLE + DEC],
                                    ident[:]).then_inc(tile_done, 1)

            def mix(c):
                job = JOB_S[c]
                s = 3 * (job % 2)
                banks_free(job)
                for h in range(2):
                    g = 2 * c + h
                    rows = slice(64 * h, 64 * h + 64)
                    for n in range(8):
                        nc.tensor.matmul(psum[rows, s + n // 4, (n % 4) * P:(n % 4 + 1) * P],
                                         v_rows[:, n, 64 * g:64 * g + 64], mix_w[:, g, :],
                                         start=True, stop=True)
                    nc.tensor.matmul(psum[rows, s + 2, DEC:DEC + P], ones[:], mix_w[:, g, :],
                                     start=True, stop=True)
                    nc.tensor.matmul(psum[rows, s + 2, 0:DEC], v_rows[0:DEC, 8, 64 * g:64 * g + 64],
                                     mix_w[0:DEC, g, 0:DEC], start=True, stop=True)
                    last = nc.tensor.matmul(psum[rows, s + 2, DEC + P:2 * DEC + P], ones[0:DEC, :],
                                            mix_w[0:DEC, g, 0:DEC], start=True, stop=True)
                last.then_inc(tile_done, 1)

            def a_rows(t):
                if t == 0:
                    pe.wait_ge(a_conv_done, 8)
                if t >= 2:
                    pe.wait_ge(row_stats, ROW_TILES + t - 1)
                n = P if t < 8 else DEC
                at_col = t * P if t < 8 else AO_SAMPLE
                for c in range(4):
                    last = nc.tensor.transpose(psum[0:n, 6 + t % 2, c * P:(c + 1) * P],
                                               a_out[c][:, at_col:at_col + n], ident[:])
                last.then_inc(a_rows_ready, 1)

            def spread_ln(n, col, job):
                b0 = 3 * ((job - 1) % 2)
                pe.wait_ge(tile_evacuated, evacuated(job - 1))
                if n == 0:
                    pe.wait_ge(neg_mean_ready, 2)
                    pe.wait_ge(row_stats, 2 * ROW_TILES)
                else:
                    pe.wait_ge(ln_copied, 1)
                for t in range(ROW_TILES):
                    k = P if t < 8 else DEC
                    out = psum[:, 6 + t // 4, (t % 4) * P:(t % 4 + 1) * P] if t < 8 else \
                        psum[:, b0, CH + 2:CH + 2 + DEC]
                    last = nc.tensor.matmul(out, col[0:k, t:t + 1].to_broadcast([k, P]), ident[0:k, 0:k],
                                            start=True, stop=True)
                last.then_inc(ln_spread, 1)

            def a_statistics(first):
                def between(m, k):
                    step = 4 * (first + m) + k
                    if ROWS_STEP <= step < ROWS_STEP + ROW_TILES:
                        a_rows(step - ROWS_STEP)
                    for n, col in enumerate((rstd, neg_mean)):
                        if step == SPREAD_STEP + 4 * n:
                            spread_ln(n, col, JOB_DOWN_B + first + m)
                        if step == SPREAD_STEP + 4 * n + 3:
                            pe.wait_ge(ln_copied, n + 1)
                return between

            pe.wait_ge(consts_made, 4)
            phase_start(0)
            for q in range(4):
                up_job(2 + q, 2 + q, q % 2, q % 2)
            up_job(6, 6, 0, 0)
            up_job(7, 7, 1, 1)
            turn_v(0)
            up_job(9, 8, 1, 0)
            turn_v(1)
            up_job(11, 9, 1, 1)
            turn_v(2)
            turn_v(3)
            up_job(14, 10, 0, 0)
            up_job(15, 11, 1, 1)
            pe.wait_ge(v_ready, ROW_TILES)
            pe.wait_ge(mask_set, 1)
            for c in range(4):
                mix(c)
                up_job(JOB_S[c] + 1, 12 + c, 1, c % 2)
            for s in range(4):
                down_jobs(JOB_DOWN_B + 2 * s, 16 + s, 0 if s == 0 else None, 0, 4, 0, s % 2,
                          between=a_statistics(2 * s), free=s == 3)
            for s in range(4):
                down_jobs(JOB_DOWN_A + 2 * s, 20 + s, 4 if s == 0 else None, 0, 4, 0, s % 2)

            def ffn(p):
                job, slab, act = JOB0[p], SLAB0[p], ACT0[p]
                s0 = job % 2
                phase_start(p)
                up_job(job + 2, slab + 2, s0, 0)
                up_job(job + 3, slab + 3, 1 - s0, 1)
                with pe.Fori(0, (FF_BLOCKS - 1) // 2) as i:
                    for q in range(2):
                        j = i * 24 + (job + 4 + 12 * q)
                        s = i * 12 + (slab + 4 + 6 * q)
                        for t in range(4):
                            up_job(j + t, s + t, (s0 + t) % 2, t % 2)
                        down_jobs(j + 4, s + 4, i * 4 + (act + 2 * q), 2 * q, 2, s0, 0)
                        down_jobs(j + 8, s + 5, None, 2 * q, 2, s0, 1)
                if p < 3:
                    j, s = job + FF_JOBS - 8, slab + FF_SLABS - 2
                    down_jobs(j, s, act + FF_TILES - 2, 0, 2, s0, 0)
                    down_jobs(j + 4, s + 1, None, 0, 2, s0, 1)

            ffn(1)
            s0 = JOB0[2] % 2
            for half in range(2):
                job, slab = JOB0[2] + 28 * half, SLAB0[2] + 16 * half
                if half == 0:
                    phase_start(2)
                for t in range(0 if half else 2, 12):
                    up_job(job + t, slab + t, (s0 + t) % 2, t % 2)
                for q in range(2):
                    down_jobs(job + 12 + 8 * q, slab + 12 + 2 * q, ACT0[2] + 4 * half + 2 * q, 2 * q, 2, s0, 0)
                    down_jobs(job + 16 + 8 * q, slab + 13 + 2 * q, None, 2 * q, 2, s0, 1)
            ffn(3)
            def chunk_stats(c):
                pe.wait_ge(squares_summed, DVE_SUMS * (5 + c))
                for t in range(3):
                    n = 3 * c + t
                    last = nc.tensor.matmul(psum[0:CH_ROWS, 7, n:n + 1], sumsq[:, n * CH_ROWS:(n + 1) * CH_ROWS],
                                            ones[:, 0:1], start=True, stop=True)
                last.then_inc(stats_ready, 1)

            def chunk_spread(c):
                if c:
                    pe.wait_ge(r_ready, 8 + c)
                pe.wait_ge(r_col_ready, 5 + c)
                for t in range(3):
                    last = nc.tensor.matmul(psum[:, 6, t * CH_ROWS:(t + 1) * CH_ROWS],
                                            r_col[:, 3 * c + t:3 * c + t + 1].to_broadcast([P, P]),
                                            ident[:, 0:CH_ROWS], start=True, stop=True)
                last.then_inc(r_spread, 1)

            for c in range(3):
                cols = slice(c * CH, (c + 1) * CH)
                for m in range(KD):
                    if c and m == 3:
                        chunk_stats(c - 1)
                    if c and m == 7:
                        chunk_spread(c - 1)
                    n = KD * c + m
                    pe.wait_ge(tile_evacuated, evacuated(FINAL_JOB + (n - 6 if n >= 6 else n // 3 - 2)))
                    if c == 0 and m in (0, 4):
                        pe.wait_ge(weights_ready, N_SLABS - 1 + m // 4)
                    for k in range(2):
                        if n == 0:
                            pe.wait_ge(act_ready, ACT0[3] + FF_TILES - 1 + k)
                        last = split_product(psum[:, n % 6, 0:CH], 2 * (m % 4) + k, m // 4, ah_t[:, k, cols],
                                             al_t[:, k, cols], k == 0, k == 1)
                    last.then_inc(tile_done, 1)
            chunk_stats(2)
            chunk_spread(2)

        @block.gpsimd
        def _(pool):
            nc.gpsimd.memset(ident[:], 0.0).then_inc(consts_made, 1)
            nc.gpsimd.memset(minus_half[:], -0.5).then_inc(consts_made, 1)
            nc.gpsimd.memset(ones[:], 1.0).then_inc(consts_made, 1)
            pool.wait_ge(consts_made, 3)
            nc.gpsimd.affine_select(out=ident[:], in_=ident[:], compare_op=ALU.not_equal, fill=1.0, base=0,
                                    pattern=[[-1, P]], channel_multiplier=1).then_inc(consts_made, 1)

            def split_lo(n, slot):
                pool.wait_ge(weights_hi, n + 1)
                s = slice(slot * SLAB, (slot + 1) * SLAB)
                nc.gpsimd.tensor_tensor(w_lo[:, s], raw[:, s], w_hi[:, s].bitcast(F32),
                                        ALU.subtract).then_inc(weights_ready, 1)

            def early_squares(p, m, cols=slice(0, COLS)):
                pool.wait_ge(square_ready, KD * p + m + 1)
                if m > 1:
                    pool.wait_ge(early_sum, POOL_SUMS * p + m - 1)
                nc.gpsimd.tensor_tensor(sumsq[:, cols], (square[0] if m == 1 else sumsq)[:, cols],
                                        square[m][:, cols], ALU.add).then_inc(early_sum, 1)

            def r_of_frames(p):
                pool.wait_ge(mean_sq_ready, p + 1)
                nc.gpsimd.tensor_tensor(r_col[:], mean_sq[:], minus_half[:], ALU.pow).then_inc(r_col_ready, 1)

            def pool_taps(c, first, end):
                for i in range(first, end):
                    if i == 0:
                        continue
                    pool.wait_ge(a_tap_product, POOL_TAPS * c + i + 1)
                    if i == 1:
                        if c >= 2:
                            pool.wait_ge(a_conv_done, 2 * (c - 1))
                        a = tap_prod[(POOL_TAPS * c) % 2]
                    else:
                        pool.wait_ge(a_pool_sum, (POOL_TAPS - 1) * c + i - 1)
                        a = pool_sum[c % 2]
                    nc.gpsimd.tensor_tensor(pool_sum[c % 2], a, tap_prod[(POOL_TAPS * c + i) % 2],
                                            ALU.add).then_inc(a_pool_sum, 1)

            def row_rstd(n):
                pool.wait_ge(var_ready, n)
                nc.gpsimd.tensor_tensor(rstd[:], var_eps[:], minus_half[:], ALU.pow).then_inc(rstd_ready, 1)

            split_lo(0, 0)
            split_lo(1, 1)
            for m in (1, 2, 3):
                early_squares(0, m)
            r_of_frames(0)
            split_lo(2, 0)
            for slot in range(2, 19):
                split_lo(slot + 1, (slot + 1) % 2)
                for c, first, end in A_PLAN.get(slot, ()):
                    pool_taps(c, first, end)
                if slot == 10:
                    row_rstd(1)
                if slot == 16 + (ROWS_STEP + ROW_TILES) // 8:
                    row_rstd(2)
            for c in (2, 3):
                pool.wait_ge(ln_copied, 1)
                nc.gpsimd.tensor_tensor(a_out[c], a_out[c], tap_prod[0], ALU.mult).then_inc(a_scaled_pool, 1)
            split_lo(20, 0)
            split_lo(21, 1)
            early_squares(1, 1)
            split_lo(22, 0)
            early_squares(1, 2)
            early_squares(1, 3)
            split_lo(23, 1)
            for p in (1, 2, 3):
                n0 = SLAB0[p]
                n1 = SLAB0[p + 1] if p < 3 else N_SLABS
                split_lo(n0, 0)
                split_lo(n0 + 1, 1)
                r_of_frames(p)
                with pool.Fori(1, (n1 - n0) // 2) as i:
                    split_lo(i * 2 + n0, 0)
                    split_lo(i * 2 + n0 + 1, 1)
                if p < 3:
                    for m in (1, 2, 3):
                        early_squares(p + 1, m)

            def chunk_r(c):
                pool.wait_ge(mean_sq_ready, 5 + c)
                nc.gpsimd.tensor_tensor(r_col[:, 3 * c:3 * c + 3], mean_sq[:, 3 * c:3 * c + 3],
                                        minus_half[:, 3 * c:3 * c + 3], ALU.pow).then_inc(r_col_ready, 1)

            def chunk_y(c):
                cols = slice(c * CH, (c + 1) * CH)
                pool.wait_ge(r_ready, 9 + c)
                for m in range(DVE_Y, KD):
                    pool.wait_ge(x_scaled, (KD - DVE_Y) * c + m - DVE_Y + 1)
                    nc.gpsimd.tensor_tensor(x_t[:, m, cols], x_t[:, m, cols], r_rows[:, cols],
                                            ALU.mult).then_inc(y_ready_pool, 1)

            for c in range(3):
                cols = slice(c * CH, (c + 1) * CH)
                early_squares(4 + c, 1, cols)
                early_squares(4 + c, 2, cols)
                if c == 2:
                    chunk_r(1)
                early_squares(4 + c, 3, cols)
                if c == 1:
                    chunk_r(0)
                    chunk_y(0)
            chunk_y(1)
            chunk_r(2)
            chunk_y(2)

        @block.scalar
        def _(act):
            def split_hi(n, slot, after):
                act.wait_ge(raw_loaded[slot], n * 8 + (16 - 8 * slot))
                if after is not None:
                    act.wait_ge(tile_done, after)
                s = slice(slot * SLAB, (slot + 1) * SLAB)
                nc.scalar.activation(w_hi[:, s], raw[:, s], ACT.Copy).then_inc(weights_hi, 1)

            def hi(n):
                split_hi(n, n % 2, AFTER[n - 2] if n >= 2 else None)

            def xg_high(p, m):
                nc.scalar.activation(hi_t[:, m, :], x_t[:, m, :], ACT.Identity,
                                     scale=cst("gain", p * KD + m)).then_inc(xg_hi_ready, 1)

            def make_xg(p, m, job):
                act.wait_ge(tile_evacuated, evacuated(job))
                xg_high(p, m)
                nc.scalar.activation(square[m], x_t[:, m, :], ACT.Square).then_inc(square_ready, 1)

            def hidden_hi(a, par, slot):
                act.wait_ge(product_done, a - ACT0[1] + 1)
                nc.scalar.activation(ah_t[:, slot, :], prod[par], ACT.Copy).then_inc(act_hi_ready, 1)

            def silu_gate(t, par):
                act.wait_ge(conv_tap, t * 3 + 3)
                nc.scalar.activation(factor[par], conv_out[par], ACT.Silu).then_inc(silu_done, 1)

            def tap_products(c, first, end):
                for i in range(first, end):
                    if i == 0:
                        act.wait_ge(const_loaded, 16)
                        act.wait_ge(glu_written, 4 * (c + 2))
                    n = POOL_TAPS - 1
                    used = n * c - 1 if i == 0 else n * c if i == 1 else n * c + max(1, i - 2)
                    if used > 0:
                        act.wait_ge(a_pool_sum, used)
                    k = DVE_TAPS + i
                    nc.scalar.activation(tap_prod[(POOL_TAPS * c + i) % 2], a_in[c][:, k:k + AO_COLS], ACT.Identity,
                                         scale=cst("conv_a_w", c * TAPS_A + k)).then_inc(a_tap_product, 1)

            def sigmoid_gate(c):
                act.wait_ge(tile_evacuated, evacuated(JOB_A[c] + 1))
                nc.scalar.activation(tmp[1], tmp[1], ACT.Sigmoid).then_inc(sigmoid_done, 1)

            def first_squares(*tiles):
                for m in tiles:
                    nc.scalar.activation(square[m], x_t[:, m, :], ACT.Square).then_inc(square_ready, 1)

            act.wait_ge(consts_made, 3)
            nc.scalar.activation(var_eps[:], ones[:, 0:ROW_TILES], ACT.Copy).then_inc(var_eps_set, 1)
            hi(0)
            act.wait_ge(gains_loaded, 16)
            for m in range(KD):
                act.wait_ge(x_loaded[m], 16)
                xg_high(0, m)
                if m == 0:
                    first_squares(0)
                if m == 2:
                    first_squares(1)
                    hi(1)
                if m == 3:
                    first_squares(2)
            first_squares(*range(3, KD))
            hi(2)

            def v_out_of_psum(c):
                job = JOB_V[c]
                act.wait_ge(tile_done, job + 1)
                if c == 0:
                    act.wait_ge(glu_written, 16)
                if c >= 2:
                    act.wait_ge(tile_done, JOB_VT[c - 2] + 1)
                nc.scalar.activation(tmp[c % 2].rearrange("p (c n) -> p c n", c=3),
                                     psum[:, 3 * (job % 2):3 * (job % 2) + 3, 0:CH],
                                     ACT.Copy).then_inc(v_evacuated, 1)

            def v_rows_out_of_psum(c):
                job = JOB_VT[c]
                s = 3 * (job % 2)
                act.wait_ge(tile_done, job + 1)
                nc.scalar.activation(v_rows[:, 0:8, c * P:(c + 1) * P],
                                     psum[:, s:s + 2, :].rearrange("p a (b f) -> p (a b) f", f=P), ACT.Copy)
                nc.scalar.activation(v_rows[0:DEC, 8, c * P:(c + 1) * P], psum[0:DEC, s + 2, 0:P],
                                     ACT.Copy).then_inc(v_evacuated, 1)

            def v_norm():
                act.wait_ge(neg_mean_ready, 1)
                for t in reversed(range(ROW_TILES)):
                    n = P if t < 8 else DEC
                    nc.scalar.activation(v_rows[0:n, t, :], v_rows[0:n, t, :], ACT.Identity,
                                         scale=rstd[0:n, t:t + 1],
                                         bias=neg_mean[0:n, t:t + 1]).then_inc(v_ready, 1)

            def b_hi(c):
                act.wait_ge(tile_evacuated, evacuated(JOB_S[c] + 1))
                nc.scalar.activation(ah_t[:, c, :], tmp[0], ACT.Copy).then_inc(act_hi_ready, 1)

            for slot in range(2, 19):
                if slot in (7, 8, 9, 10):
                    v_out_of_psum(slot - 7)
                if slot == 10:
                    v_rows_out_of_psum(2)
                hi(slot + 1)
                if slot in (2, 4, 6):
                    sigmoid_gate(slot // 2 - 1)
                if slot in (8, 9):
                    v_rows_out_of_psum(slot - 8)
                if slot == 10:
                    v_rows_out_of_psum(3)
                if slot == 12:
                    sigmoid_gate(3)
                if slot in (13, 14, 15, 16):
                    b_hi(slot - 13)
                for c, first, end in A_PLAN.get(slot, ()):
                    tap_products(c, first, end)
                if slot == 10:
                    v_norm()

            def ln_out_of_psum(n, b0):
                dst = tap_prod[n]
                act.wait_ge(ln_spread, n + 1)
                nc.scalar.activation(dst[:, 0:SEQ], psum[:, 6:8, :].rearrange("p a b -> p (a b)"), ACT.Copy)
                nc.scalar.activation(dst[:, AO_SAMPLE:AO_SAMPLE + DEC], psum[:, b0, CH + 2:CH + 2 + DEC],
                                     ACT.Copy).then_inc(ln_copied, 1)

            ln_out_of_psum(0, 0)
            hi(20)
            ln_out_of_psum(1, 3)
            def a_silu(c):
                act.wait_ge(a_normed, c + 1)
                nc.scalar.activation(a_out[c], a_out[c], ACT.Silu, scale=cst("ln_a_g", c),
                                     bias=cst("ln_a_b", c)).then_inc(a_silu_done, 1)

            a_silu(0)
            a_silu(1)
            for c in range(4):
                if 1 <= c <= 2:
                    a_silu(c + 1)
                act.wait_ge(a_silu_done, c + 1)
                if c < 3:
                    act.wait_ge(act_free, c + 1)
                else:
                    act.wait_ge(tile_done, JOB_DOWN_A)
                nc.scalar.activation(ah_t[:, c, 0:SEQ], a_out[c][:, 0:SEQ], ACT.Copy)
                nc.scalar.activation(ah_t[:, c, SAMPLE:SAMPLE + DEC], a_out[c][:, AO_SAMPLE:AO_SAMPLE + DEC],
                                     ACT.Copy).then_inc(act_hi_ready, 1)
            for s in range(4):
                hi(21 + s)
                for m in (2 * s, 2 * s + 1):
                    make_xg(1, m, JOB_DOWN_A + m)

            def last_down(p, job, slab):
                hi(slab + 1)
                for m in range(4):
                    make_xg(p + 1, m, job + m)
                hi(slab + 2)
                for m in range(4, 8):
                    make_xg(p + 1, m, job + m)

            def ffn(p):
                job, slab, a0, t0 = JOB0[p], SLAB0[p], ACT0[p], CONV0[p]
                for q in range(2):
                    hi(slab + 1 + 2 * q)
                    hi(slab + 2 + 2 * q)
                    silu_gate(t0 + q, q)
                    hidden_hi(a0 + q, q, q)
                with act.Fori(0, (FF_BLOCKS - 1) // 2) as i:
                    for b in range(2):
                        for step in range(6):
                            n = slab + 5 + 6 * b + step
                            split_hi(i * 12 + n, n % 2, i * 24 + AFTER[n - 2])
                            f = 2 * b + step // 2
                            if step in (1, 3):
                                silu_gate(i * 4 + (t0 + 2 + f), f % 2)
                            if step in (2, 4):
                                f = 2 * b + step // 2 - 1
                                hidden_hi(i * 4 + (a0 + 2 + f), f % 2, (2 + f) % 4)
                if p < 3:
                    last_down(p, job + FF_JOBS - 8, slab + FF_SLABS - 2)

            ffn(1)
            for half in range(2):
                job, slab, a0 = JOB0[2] + 28 * half, SLAB0[2] + 16 * half, ACT0[2] + 4 * half
                for t in range(4):
                    hi(slab + 3 * t + 1)
                    hi(slab + 3 * t + 2)
                    hi(slab + 3 * t + 3)
                    hidden_hi(a0 + t, t % 2, t)
                hi(slab + 13)
                hi(slab + 14)
                if half == 0:
                    hi(slab + 15)
                    hi(slab + 16)
                else:
                    last_down(2, job + 20, slab + 14)
            ffn(3)
            hi(N_SLABS - 1)
            for c in range(3):
                cols = slice(c * CH, (c + 1) * CH)
                for m in range(KD):
                    act.wait_ge(tile_evacuated, evacuated(FINAL_JOB + KD * c + m))
                    nc.scalar.activation(square[m][:, cols], x_t[:, m, cols], ACT.Square).then_inc(square_ready, 1)
                    if m >= DVE_Y:
                        act.wait_ge(square_ready, KD * (4 + c) + m + 1)
                        nc.scalar.activation(x_t[:, m, cols], x_t[:, m, cols], ACT.Identity,
                                             scale=cst("gain", 4 * KD + m)).then_inc(x_scaled, 1)

        @block.vector
        def _(dve):
            def tile3(pset):
                return psum[:, 3 * pset:3 * pset + 3, 0:CH]

            def cols3(ap):
                return ap.rearrange("p (c n) -> p c n", c=3)

            def times_r(job, pset, out):
                dve.wait_ge(tile_done, job + 1)
                dve.tensor_tensor(cols3(out), tile3(pset), r_3, ALU.mult).then_inc(tile_evacuated, 1)

            def late_squares(p, m, cols=slice(0, COLS)):
                n = DVE_SUMS * p
                dve.wait_ge(square_ready, KD * p + m + 1)
                if m > 5:
                    dve.wait_ge(squares_summed, n + m - 5)
                part = square[4][:, cols]
                dve.tensor_tensor(part, part, square[m][:, cols], ALU.add).then_inc(squares_summed, 1)
                if m == KD - 1:
                    dve.wait_ge(squares_summed, n + 3)
                    dve.wait_ge(early_sum, POOL_SUMS * (p + 1))
                    dve.tensor_tensor(sumsq[:, cols], sumsq[:, cols], part, ALU.add).then_inc(squares_summed, 1)

            def xg_low(p, m):
                dve.wait_ge(xg_hi_ready, KD * p + m + 1)
                dve.scalar_tensor_tensor(lo_t[:, m, :], x_t[:, m, :], cst("gain", p * KD + m),
                                         hi_t[:, m, :].bitcast(F32), ALU.mult,
                                         ALU.subtract).then_inc(xg_ready, 1)

            def clear_pad():
                dve.memset(sumsq[:, COLS:ROW_TILES * P], 0.0).then_inc(pad_cleared, 1)

            def add_down(job, pset, m, loaded=None):
                if loaded is not None:
                    dve.wait_ge(x_loaded[m], loaded)
                dve.wait_ge(tile_done, job + 1)
                dve.wait_ge(tile_evacuated, evacuated(job - 1))
                dve.tensor_tensor(cols3(x_t[:, m, :]), tile3(pset), cols3(x_t[:, m, :]),
                                  ALU.add).then_inc(tile_evacuated, 1)

            def last_down(p, job, pset):
                clear_pad()
                for m in range(KD):
                    add_down(job + m, (pset + m) % 2, m)
                    if m >= 1:
                        xg_low(p + 1, m - 1)
                    if m >= 6:
                        late_squares(p + 1, m - 1)
                xg_low(p + 1, KD - 1)
                late_squares(p + 1, KD - 1)

            def rms(p, tail):
                dve.wait_ge(stats_ready, p + 1)
                dve.tensor_scalar(mean_sq[:], psum[:, tail, CH + 2:CH + 2 + ROW_TILES], 1.0 / D, EPS, ALU.mult,
                                  ALU.add).then_inc(mean_sq_ready, 1)
                dve.wait_ge(r_spread, p + 1)
                dve.tensor_copy(r_rows[:, 0:1024], psum[:, 6:8, :].rearrange("p a b -> p (a b)")).then_inc(r_ready, 1)
                dve.tensor_copy(r_rows[:, 1024:COLS],
                                psum[:, tail, CH + 30:CH + 30 + COLS - 1024]).then_inc(r_ready, 1)
                dve.wait_ge(r_ready, 2 * (p + 1))

            def conv3(t, par, w_at, w_name, state_at, state_name, new, new_at):
                g = conv_in[par]
                last_frames = g[:, 992:1060].rearrange("p (a b) -> p a b", b=34)[:, :, 32:34]
                dve.tensor_scalar(new[:, bass.ds(new_at, 4)].rearrange("p (a b) -> p a b", a=2), last_frames,
                                  1.0, None, ALU.mult).then_inc(state_saved, 1)
                dve.tensor_scalar(g[:, SAMPLE:SAMPLE + 2], cst(state_name, state_at, 2), 1.0, None,
                                  ALU.mult).then_inc(history_set, 1)
                dve.wait_ge(history_set, t + 1)
                dve.tensor_scalar(conv_out[par], g[:, 0:COLS], cst(w_name, w_at), None,
                                  ALU.mult).then_inc(conv_tap, 1)
                for k in (1, 2):
                    dve.wait_ge(conv_tap, t * 3 + k)
                    dve.scalar_tensor_tensor(conv_out[par], g[:, k:k + COLS], cst(w_name, w_at + k), conv_out[par],
                                             ALU.mult, ALU.add).then_inc(conv_tap, 1)

            def hidden_lo(a, par, slot):
                dve.wait_ge(act_hi_ready, a + 1)
                dve.tensor_tensor(al_t[:, slot, :], prod[par], ah_t[:, slot, :].bitcast(F32),
                                  ALU.subtract).then_inc(act_ready, 1)

            dve.wait_ge(gains_loaded, 16)
            clear_pad()
            dve.memset(mv[:], 0.0).then_inc(pad_cleared, 1)
            for m in range(KD):
                xg_low(0, m)
            for m in range(5, KD):
                late_squares(0, m)
            dve.wait_ge(squares_summed, DVE_SUMS)
            for c in range(4):
                dve.memset(a_in[c][:, 0:HA], 0.0).then_inc(glu_written, 1)
            dve.wait_ge(stats_ready, 1)
            dve.tensor_scalar(mean_sq_s[0:DEC, :], psum[0:DEC, 0, CH + 20:CH + 21], 1.0 / D, EPS, ALU.mult, ALU.add)
            rms(0, 0)

            def tap(c, k):
                acc_s = conv_s[:, c * DEC:(c + 1) * DEC]
                if k < DVE_TAPS:
                    w = cst("conv_a_w", c * TAPS_A + k)
                    src, src_s = a_in[c][:, k:k + SEQ], a_in[c][:, AO_SAMPLE + k:AO_SAMPLE + k + DEC]
                if k == 0:
                    dve.wait_ge(glu_written, 4 * (c + 2))
                    if c:
                        dve.wait_ge(a_conv_done, 2 * c)
                    b = cst("conv_a_b", c)
                    dve.tensor_scalar(conv_acc, src, w, b, ALU.mult, ALU.add).then_inc(a_tap, 1)
                    dve.tensor_scalar(acc_s, src_s, w, b, ALU.mult, ALU.add).then_inc(a_acc_s, 1)
                elif k < DVE_TAPS:
                    dve.wait_ge(a_tap, DVE_TAPS * c + k)
                    dve.scalar_tensor_tensor(conv_acc, src, w, conv_acc, ALU.mult, ALU.add).then_inc(a_tap, 1)
                    dve.wait_ge(a_acc_s, DVE_TAPS * c + k)
                    dve.scalar_tensor_tensor(acc_s, src_s, w, acc_s, ALU.mult, ALU.add).then_inc(a_acc_s, 1)
                else:
                    dve.wait_ge(a_tap, DVE_TAPS * (c + 1))
                    dve.wait_ge(a_acc_s, DVE_TAPS * (c + 1))
                    dve.wait_ge(a_pool_sum, (POOL_TAPS - 1) * (c + 1))
                    part = pool_sum[c % 2]
                    dve.tensor_tensor(a_out[c][:, 0:SEQ], conv_acc, part[:, 0:SEQ], ALU.add).then_inc(a_conv_done, 1)
                    dve.tensor_tensor(a_out[c][:, AO_SAMPLE:AO_SAMPLE + DEC], acc_s,
                                      part[:, AO_SAMPLE:AO_SAMPLE + DEC], ALU.add).then_inc(a_conv_done, 1)

            def taps(first, end):
                for step in range(first, end):
                    tap(step // (DVE_TAPS + 1), step % (DVE_TAPS + 1))

            def glu(c):
                a = a_in[c]
                dve.wait_ge(sigmoid_done, c + 1)
                dve.tensor_tensor(a[:, HA:HA + SEQ], tmp[0][:, 0:SEQ], tmp[1][:, 0:SEQ],
                                  ALU.mult).then_inc(glu_written, 1)
                dve.tensor_tensor(a[:, A_COLS - DEC:A_COLS], tmp[0][:, SAMPLE:SAMPLE + DEC],
                                  tmp[1][:, SAMPLE:SAMPLE + DEC], ALU.mult).then_inc(glu_written, 1)
                if c == 0:
                    dve.wait_ge(const_loaded, 16)
                dve.tensor_copy(a[:, HA + SEQ:HA + SEQ + HA], cst("state_a", c * HA, HA)).then_inc(glu_written, 1)
                dve.wait_ge(glu_written, 4 + 4 * c + 3)
                last_frames = a[:, 992:A_COLS].rearrange("p (a b) -> p a b", b=62)[:, :, 32:62]
                dve.tensor_copy(new_a[:, c * 2 * HA:(c + 1) * 2 * HA].rearrange("p (a b) -> p a b", a=2),
                                last_frames).then_inc(glu_written, 1)

            mv_t = mv[:].rearrange("p (t s) -> p t s", s=2)

            def row_moment(seen, t, rows):
                n = P if t < 8 else DEC
                dve.bn_stats(bn[0:n, 6 * t:6 * t + 6], rows).then_inc(row_stats, 1)
                dve.wait_ge(row_stats, seen + 1)
                dve.bn_aggr(mv[0:n, 2 * t:2 * t + 2], bn[0:n, 6 * t:6 * t + 6]).then_inc(row_moments, 1)

            def neg_mean_rstd(n):
                dve.wait_ge(rstd_ready, n)
                dve.scalar_tensor_tensor(neg_mean[:], mv_t[:, :, 0], -1.0, rstd[:], ALU.mult,
                                         ALU.mult).then_inc(neg_mean_ready, 1)

            def v_statistics():
                dve.wait_ge(v_evacuated, 8)
                dve.wait_ge(pad_cleared, 2)
                dve.wait_ge(var_eps_set, 1)
                for t in range(ROW_TILES):
                    row_moment(t, t, v_rows[0:P if t < 8 else DEC, t, :])
                dve.wait_ge(row_moments, ROW_TILES)
                dve.scalar_tensor_tensor(var_eps[:, 0:8], mean_sq[:, 0:8], EPS, mv_t[:, 0:8, 1], ALU.mult, ALU.add)
                dve.scalar_tensor_tensor(var_eps[0:DEC, 8:9], mean_sq_s[0:DEC, :], EPS, mv_t[0:DEC, 8:9, 1],
                                         ALU.mult, ALU.add).then_inc(var_ready, 1)

            def v_sample():
                dve.wait_ge(v_ready, ROW_TILES)
                dve.wait_ge(mix_loaded, 48)
                dve.tensor_tensor(lnv_g, lnv_g, v_rows[0:DEC, 8, :], ALU.mult).then_inc(v_sample_ready, 1)
                dve.wait_ge(v_sample_ready, 1)
                dve.tensor_tensor(lnv_g, lnv_g, lnv_b, ALU.add).then_inc(v_sample_ready, 1)

            def mixed(c):
                s = 3 * (JOB_S[c] % 2)
                g, b = cst("ln_v_g", c), cst("ln_v_b", c)
                dve.wait_ge(tile_done, JOB_S[c] + 1)
                dve.scalar_tensor_tensor(mix_bias[:, 0:P], psum[:, s + 2, DEC:DEC + P], b, mix_b[:, c, :],
                                         ALU.mult, ALU.add).then_inc(mix_bias_ready, 1)
                dve.scalar_tensor_tensor(mix_bias[:, P:P + DEC], psum[:, s + 2, DEC + P:2 * DEC + P], b,
                                         mix_b[:, c, 0:DEC], ALU.mult, ALU.add).then_inc(mix_bias_ready, 1)
                dve.wait_ge(mix_bias_ready, 2 * (c + 1))
                dve.scalar_tensor_tensor(tmp[1][:, 0:SEQ].rearrange("p (n i) -> p n i", i=P),
                                         psum[:, s:s + 2, :].rearrange("p a (b i) -> p (a b) i", i=P), g,
                                         mix_bias[:, 0:P].rearrange("p (a i) -> p a i", a=1).to_broadcast([P, 8, P]),
                                         ALU.mult, ALU.add)
                dve.scalar_tensor_tensor(tmp[1][:, SAMPLE:SAMPLE + DEC], psum[:, s + 2, 0:DEC], g,
                                         mix_bias[:, P:P + DEC], ALU.mult, ALU.add).then_inc(tile_evacuated, 1)
                dve.wait_ge(tile_evacuated, evacuated(JOB_S[c]))
                dve.tensor_tensor(tmp[1], tmp[1], r_rows[:], ALU.mult).then_inc(mix_times_r, 1)

            def gated_b(c):
                job = JOB_S[c] + 1
                dve.wait_ge(tile_done, job + 1)
                dve.wait_ge(mix_times_r, c + 1)
                dve.tensor_tensor(cols3(tmp[0]), tile3(job % 2), cols3(tmp[1]),
                                  ALU.mult).then_inc(tile_evacuated, 1)

            def b_low(c):
                dve.wait_ge(act_hi_ready, c + 1)
                dve.tensor_tensor(al_t[:, c, :], tmp[0], ah_t[:, c, :].bitcast(F32),
                                  ALU.subtract).then_inc(act_ready, 1)

            times_r(0, 0, tmp[0])
            times_r(1, 1, tmp[1])
            glu(0)
            taps(0, 3)
            times_r(2, 0, tmp[0])
            taps(3, 9)
            times_r(3, 1, tmp[1])
            taps(9, 11)
            glu(1)
            taps(11, 14)
            times_r(4, 0, tmp[0])
            taps(14, 20)
            times_r(5, 1, tmp[1])
            taps(20, 22)
            glu(2)
            dve.wait_ge(mix_loaded, 48)
            dve.memset(mix_w[64:P, :, 0:64], 0.0).then_inc(mask_set, 1)
            taps(22, 51)
            v_statistics()
            taps(51, 53)
            neg_mean_rstd(1)
            times_r(14, 0, tmp[0])
            taps(53, 58)
            v_sample()
            times_r(15, 1, tmp[1])
            taps(58, 60)
            glu(3)
            for c in range(4):
                step = 60 + 6 * c
                mixed(c)
                taps(step, step + 5)
                gated_b(c)
                if c < 3:
                    taps(step + 5, step + 6)
                b_low(c)
            taps(83, 84)
            add_down(JOB_DOWN_B, 0, 0, loaded=32)
            taps(84, 4 * (DVE_TAPS + 1))
            add_down(JOB_DOWN_B + 1, 1, 1, loaded=32)
            for t in range(ROW_TILES):
                dve.wait_ge(a_rows_ready, t + 1)
                row_moment(ROW_TILES + t, t, psum[0:P if t < 8 else DEC, 6 + t % 2, :])
                m = (ROWS_STEP + t) // 4
                if (ROWS_STEP + t) % 4 == 3:
                    add_down(JOB_DOWN_B + m, m % 2, m, loaded=32)
            dve.wait_ge(row_moments, 2 * ROW_TILES)
            dve.tensor_scalar(var_eps[:], mv_t[:, :, 1], EPS, None, ALU.add).then_inc(var_ready, 1)
            neg_mean_rstd(2)

            def a_scale(c):
                dve.wait_ge(ln_copied, 1)
                dve.tensor_tensor(a_out[c], a_out[c], tap_prod[0], ALU.mult).then_inc(a_scaled, 1)

            def a_shift(c):
                if c < 2:
                    dve.wait_ge(a_scaled, c + 1)
                else:
                    dve.wait_ge(a_scaled_pool, c - 1)
                dve.wait_ge(ln_copied, 2)
                dve.tensor_tensor(a_out[c], a_out[c], tap_prod[1], ALU.add).then_inc(a_normed, 1)

            def a_low(c):
                dve.wait_ge(act_hi_ready, 4 + c + 1)
                dve.tensor_tensor(al_t[:, c, 0:SEQ], a_out[c][:, 0:SEQ], ah_t[:, c, 0:SEQ].bitcast(F32),
                                  ALU.subtract)
                dve.tensor_tensor(al_t[:, c, SAMPLE:SAMPLE + DEC], a_out[c][:, AO_SAMPLE:AO_SAMPLE + DEC],
                                  ah_t[:, c, SAMPLE:SAMPLE + DEC].bitcast(F32), ALU.subtract).then_inc(act_ready, 1)

            add_down(JOB_DOWN_B + 4, 0, 4, loaded=32)
            add_down(JOB_DOWN_B + 5, 1, 5, loaded=32)
            a_scale(0)
            a_scale(1)
            a_shift(0)
            a_shift(1)
            add_down(JOB_DOWN_B + 6, 0, 6, loaded=32)
            a_shift(2)
            a_low(0)
            a_shift(3)
            for c in range(1, 4):
                a_low(c)
            add_down(JOB_DOWN_B + 7, 1, 7, loaded=32)
            last_down(0, JOB_DOWN_A, 0)

            def clear_history():
                for g in conv_in:
                    dve.memset(g[:, 0:2], 0.0)

            def gate_tile(l, job, pset, t, f, par):
                times_r(job, pset, conv_in[par][:, 2:])
                dve.wait_ge(tile_evacuated, evacuated(job))
                at_f = f + l * FF_TILES
                conv3(t, par, at_f * 3, "conv_f_w", at_f * 2, "state_f", new_f, at_f * 4)

            def up_tile(job, pset, s, par):
                times_r(job, pset, prod[par])
                dve.wait_ge(tile_evacuated, evacuated(job))
                dve.wait_ge(silu_done, s + 1)
                dve.tensor_tensor(prod[par], prod[par], factor[par], ALU.mult).then_inc(product_done, 1)

            def ffn(p):
                l = (p - 1) // 2
                job, a0, t0 = JOB0[p], ACT0[p], CONV0[p]
                f0 = l * FF_TILES
                s0 = job % 2
                rms(p, 3 * s0)
                clear_history()
                gate_tile(l, job, s0, t0, 0, 0)
                up_tile(job + 1, 1 - s0, f0, 0)
                hidden_lo(a0, 0, 0)
                gate_tile(l, job + 2, s0, t0 + 1, 1, 1)
                up_tile(job + 3, 1 - s0, f0 + 1, 1)
                hidden_lo(a0 + 1, 1, 1)
                with dve.Fori(0, (FF_BLOCKS - 1) // 2) as i:
                    for b in range(2):
                        j = i * 24 + (job + 4 + 12 * b)
                        for q in range(2):
                            f = 2 + 2 * b + q
                            gate_tile(l, j + 2 * q, s0, i * 4 + (t0 + f), i * 4 + f, q)
                            up_tile(j + 2 * q + 1, 1 - s0, i * 4 + (f0 + f), q)
                            if q == 0:
                                hidden_lo(i * 4 + (a0 + f), q, f % 4)
                        add_down(j + 4, s0, 0)
                        hidden_lo(i * 4 + (a0 + 3 + 2 * b), 1, (3 + 2 * b) % 4)
                        for m in range(1, KD):
                            add_down(j + 4 + m, (s0 + m) % 2, m)
                if p < 3:
                    last_down(p, job + FF_JOBS - 8, s0)

            ffn(1)
            p = 2
            s0 = JOB0[p] % 2
            rms(p, 3 * s0)
            clear_history()

            def c_tile(job, c):
                par = c % 2
                sets = [(job + q) % 2 for q in range(3)]
                times_r(job, sets[0], factor[par])
                times_r(job + 1, sets[1], prod[par])
                dve.wait_ge(tile_evacuated, evacuated(job + 1))
                dve.tensor_tensor(conv_in[par][:, 2:], factor[par], prod[par], ALU.mult).then_inc(factor_ready, 1)
                dve.wait_ge(factor_ready, c + 1)
                conv3(CONV0[p] + c, par, c * 3, "conv_c_w", c * 2, "state_c", new_c, c * 4)
                times_r(job + 2, sets[2], prod[par])
                dve.wait_ge(tile_evacuated, evacuated(job + 2))
                dve.wait_ge(conv_tap, 3 * (CONV0[p] + c + 1))
                dve.tensor_tensor(prod[par], prod[par], conv_out[par], ALU.mult).then_inc(product_done, 1)

            for half in range(2):
                job = JOB0[p] + 28 * half
                for t in range(4):
                    c = 4 * half + t
                    c_tile(job + 3 * t, c)
                    if t < 3:
                        hidden_lo(ACT0[p] + c, c % 2, t)
                for m in range(KD):
                    add_down(job + 12 + m, (s0 + m) % 2, m)
                    if m == 0:
                        hidden_lo(ACT0[p] + 4 * half + 3, 1, 3)
                if half == 0:
                    for m in range(KD):
                        add_down(job + 20 + m, (s0 + m) % 2, m)
                else:
                    last_down(p, job + 20, s0)
            ffn(3)
            def chunk_add(c, m):
                cols = slice(c * CH, (c + 1) * CH)
                n = KD * c + m
                dve.wait_ge(tile_done, FINAL_JOB + n + 1)
                dve.wait_ge(tile_evacuated, evacuated(FINAL_JOB - 1))
                dve.tensor_tensor(x_t[:, m, cols], psum[:, n % 6, 0:CH], x_t[:, m, cols],
                                  ALU.add).then_inc(tile_evacuated, 1)

            def chunk_mean_square(c):
                dve.wait_ge(stats_ready, 5 + c)
                dve.tensor_scalar(mean_sq[0:CH_ROWS, 3 * c:3 * c + 3], psum[0:CH_ROWS, 7, 3 * c:3 * c + 3],
                                  1.0 / D, EPS, ALU.mult, ALU.add).then_inc(mean_sq_ready, 1)

            def chunk_r(c):
                dve.wait_ge(r_spread, 5 + c)
                dve.tensor_copy(r_rows[:, c * CH:(c + 1) * CH], psum[:, 6, 0:CH]).then_inc(r_ready, 1)
                dve.wait_ge(r_ready, 9 + c)

            def chunk_y(c, first, end):
                cols = slice(c * CH, (c + 1) * CH)
                for m in range(first, end):
                    dve.scalar_tensor_tensor(x_t[:, m, cols], x_t[:, m, cols], cst("gain", 4 * KD + m),
                                             r_rows[:, cols], ALU.mult, ALU.mult).then_inc(y_ready, 1)

            for c in range(3):
                cols = slice(c * CH, (c + 1) * CH)
                for m in range(KD):
                    chunk_add(c, m)
                    if c and m == 0:
                        late_squares(3 + c, KD - 1, slice((c - 1) * CH, c * CH))
                    if c and m == 3:
                        chunk_mean_square(c - 1)
                    if c == 2 and 1 <= m <= DVE_Y:
                        chunk_y(0, m - 1, m)
                    if m >= 6:
                        late_squares(4 + c, m - 1, cols)
                    if c and m == 6:
                        chunk_r(c - 1)
            late_squares(6, KD - 1, cols)
            chunk_y(1, 0, 2)
            chunk_mean_square(2)
            chunk_y(1, 2, DVE_Y)
            chunk_r(2)
            chunk_y(2, 0, DVE_Y)


A_PLAN = {2: [(0, 0, 3)], 3: [(0, 3, 6)], 4: [(0, 6, 9)], 5: [(0, 9, 10), (1, 0, 3)], 6: [(1, 3, 6)],
          7: [(1, 6, 9)], 8: [(1, 9, 10), (2, 0, 3)], 9: [(2, 3, 6)], 10: [(2, 6, 8)], 11: [(2, 8, 10)],
          12: [(3, 0, 3)], 13: [(3, 3, 6)], 14: [(3, 6, 9)], 15: [(3, 9, 10)]}


def _pack(inputs):
    def cols(a):
        a = np.asarray(a)
        lead = a.reshape(-1, a.shape[-1] // P, P)
        return lead.transpose(2, 1, 0).reshape(P, -1)

    i = {k: np.asarray(v) for k, v in inputs.items()}
    xt = np.zeros((D, COLS), np.float32)
    xt[:, 0:SEQ] = i["x_prompt"][0].T
    xt[:, SAMPLE:SAMPLE + DEC] = i["x_sample"][0].T

    def up(w, t):
        return w[:, t * P:(t + 1) * P].reshape(KD, P, P).transpose(1, 0, 2).reshape(P, SLAB)

    def down(w, row, n_k, s):
        n_m = 8 // n_k
        part = w[row:row + n_k * P, s * n_m * P:(s + 1) * n_m * P]
        return part.reshape(n_k, P, n_m, P).transpose(1, 2, 0, 3).reshape(P, SLAB)

    slabs = []
    w, wo = i["w_in_ab"][0], i["w_out_ab"][0]
    order = [0, 4, 1, 5, 2, 6] + [12, 13, 14, 15] + [3, 7] + [8, 9, 10, 11]
    slabs += [up(w, t) for t in order]
    slabs += [down(wo, AW, 4, s) for s in range(4)] + [down(wo, 0, 4, s) for s in range(4)]

    def ffn(l):
        w, wd = i["w_up"][l], i["w_down"][l]
        for b in range(FF_BLOCKS):
            for f in (2 * b, 2 * b + 1):
                slabs.extend([up(w, f), up(w, FF_TILES + f)])
            if b:
                slabs.extend(down(wd, 2 * (b - 1) * P, 2, s) for s in range(2))
        slabs.extend(down(wd, 2 * (FF_BLOCKS - 1) * P, 2, s) for s in range(2))

    ffn(0)
    w, wo = i["w_in_c"][0], i["w_out_c"][0]
    for half in range(2):
        for c in range(4 * half, 4 * half + 4):
            slabs += [up(w, KD + c), up(w, 2 * KD + c), up(w, c)]
        for b in (2 * half, 2 * half + 1):
            slabs += [down(wo, 2 * b * P, 2, s) for s in range(2)]
    ffn(1)
    slabs = np.stack(slabs)
    assert slabs.shape[0] == N_SLABS

    gains = [i["norm_mix"][0], i["norm_ffn"][0], i["norm_mix"][1], i["norm_ffn"][1], i["norm_final"]]
    parts = {
        "gain": np.concatenate([cols(g) for g in gains], 1),
        "conv_a_w": cols(i["conv_a_w"][0]), "conv_a_b": cols(i["conv_a_b"][0]),
        "ln_v_g": cols(i["ln_v_g"][0]), "ln_v_b": cols(i["ln_v_b"][0]),
        "ln_a_g": cols(i["ln_a_g"][0]), "ln_a_b": cols(i["ln_a_b"][0]), "state_a": cols(i["state_conv_a"][0, 0]),
        "conv_c_w": cols(i["conv_c_w"][0]), "state_c": cols(i["state_conv_c"][0, 0]),
        "conv_f_w": np.concatenate([cols(i["conv_f_w"][l]) for l in range(2)], 1),
        "state_f": np.concatenate([cols(i["state_ffn"][l, 0]) for l in range(2)], 1),
    }
    consts = np.concatenate([parts[n] for n, _ in _SIZES], 1)
    assert consts.shape == (P, N_CONST)
    mix = i["ws_b"][0].transpose(2, 0, 1).reshape(P, 8 * P)
    bs = np.repeat(i["bs_b"][0].reshape(4, 2, P), 64, axis=1)
    bs = bs.transpose(1, 0, 2).reshape(P, 4 * P)
    lnv = np.tile(np.concatenate([i["ln_v_g"][0], i["ln_v_b"][0]])[None], (DEC, 1))
    return [("x_t", xt), ("slabs", slabs), ("consts", consts), ("mix", mix), ("bs", bs), ("lnv", lnv)]


_OUTS = [("y_t", (D, COLS)), ("a_state", (P, 4 * 2 * HA)), ("c_state", (P, KD * 4)),
         ("f_state", (P, 2 * FF_TILES * 4)), ("v_rows_out", (DEC, AW))]


def kernel(**inputs):
    import concourse.bacc as bacc
    from concourse.bass_utils import run_bass_kernel_spmd

    nc = bacc.Bacc("TRN2", target_bir_lowering=False, num_devices=1)
    arrays, args = {}, []
    for name, a in _pack(inputs):
        a = np.ascontiguousarray(a)
        arrays[name] = a
        args.append(nc.dram_tensor(name, a.shape, mybir.dt.from_np(a.dtype), kind="ExternalInput").ap())
    for name, shape in _OUTS:
        args.append(nc.dram_tensor(name, shape, F32, kind="ExternalOutput").ap())
    build(nc, *args)
    got = run_bass_kernel_spmd(nc, [arrays], core_ids=[0]).results[0]

    def rows(a, tiles, n):
        a = np.asarray(a).reshape(P, tiles, 2, n).transpose(2, 3, 1, 0).reshape(2, n, tiles * P)
        return a[0], a[1]

    y = np.asarray(got["y_t"])
    y_prompt = np.ascontiguousarray(y[:, 0:SEQ].T)[None]
    y_sample = np.ascontiguousarray(y[:, SAMPLE:SAMPLE + DEC].T)[None]
    a_p, a_s = rows(got["a_state"], 4, HA)
    c_p, c_s = rows(got["c_state"], KD, 2)
    f = np.asarray(got["f_state"]).reshape(P, 2, FF_TILES * 4)
    f_ps = [rows(np.ascontiguousarray(f[:, l]), FF_TILES, 2) for l in range(2)]
    f_p = np.stack([q[0][None] for q in f_ps])
    f_s = np.stack([q[1][None] for q in f_ps])
    v = np.asarray(got["v_rows_out"])[None, None]
    return (y_prompt, y_sample, a_p[None, None], a_s[None, None], c_p[None, None], c_s[None, None], f_p, f_s, v)
```
